# Optimizing a Trainium2 kernel written in Bass

```python
import jax, jax.numpy as jnp
from jax import lax
import numpy as np

D_MODEL = 1024
BATCH = 1
SEQ = 512
DEPTH = 2

CHUNK = 64
Q_BLOCK = 128
HEAD_DIM = 64
A_HEADS = D_MODEL // HEAD_DIM
A_KV_HEADS = 4
IDX_HEADS = 8
IDX_DIM = 64
TOPK_MAX = 256
B_HEADS = D_MODEL // HEAD_DIM
D_FF = 4 * D_MODEL
ROPE_THETA = 10000.0
EPS = 1e-6
N_A = DEPTH // 2
N_B = DEPTH - N_A

A_Q = A_HEADS * HEAD_DIM
A_KV = A_KV_HEADS * HEAD_DIM
A_QI = IDX_HEADS * IDX_DIM
A_IN = A_Q + 2 * A_KV + A_QI + IDX_DIM + IDX_HEADS
A_SPLITS = [A_Q, A_Q + A_KV, A_Q + 2 * A_KV, A_Q + 2 * A_KV + A_QI, A_Q + 2 * A_KV + A_QI + IDX_DIM]
B_QK = B_HEADS * HEAD_DIM
B_KV_IN = 2 * B_QK + B_HEADS


def rms_norm(x, g):
    x32 = x.astype(jnp.float32)
    y = x32 * lax.rsqrt(jnp.mean(x32 * x32, axis=-1, keepdims=True) + EPS)
    return (y * g.astype(jnp.float32)).astype(x.dtype)

def apply_rope(x):
    s, d = x.shape[1], x.shape[-1]
    half = d // 2
    inv = 1.0 / (ROPE_THETA ** (jnp.arange(0, d, 2, dtype=jnp.float32) / d))
    ang = jnp.arange(s, dtype=jnp.float32)[:, None] * inv[None, :]
    c = jnp.cos(ang)[None, :, None, :]
    sn = jnp.sin(ang)[None, :, None, :]
    x1 = x[..., :half].astype(jnp.float32)
    x2 = x[..., half:].astype(jnp.float32)
    return jnp.concatenate([x1 * c - x2 * sn, x1 * sn + x2 * c], axis=-1).astype(x.dtype)

def to_blocks(a):
    b, s = a.shape[:2]
    return jnp.moveaxis(a.reshape(b, s // Q_BLOCK, Q_BLOCK, *a.shape[2:]), 1, 0)

def from_blocks(a):
    a = jnp.moveaxis(a, 0, 1)
    return a.reshape(a.shape[0], a.shape[1] * a.shape[2], *a.shape[3:])

def dsa_attention(xn, w_in, w_o):
    b, s, _ = xn.shape
    q, k, v, qi, ki, wi = jnp.split(xn @ w_in, A_SPLITS, axis=-1)
    q = apply_rope(q.reshape(b, s, A_HEADS, HEAD_DIM))
    k = apply_rope(k.reshape(b, s, A_KV_HEADS, HEAD_DIM))
    v = v.reshape(b, s, A_KV_HEADS, HEAD_DIM)
    qi = apply_rope(qi.reshape(b, s, IDX_HEADS, IDX_DIM))
    ki = apply_rope(ki[:, :, None, :])[:, :, 0]
    wi = wi * (IDX_HEADS ** -0.5 * IDX_DIM ** -0.5)
    n_sel = min(TOPK_MAX, s // 4)
    key_pos = jnp.arange(s)
    t_pos = key_pos.reshape(s // Q_BLOCK, Q_BLOCK)
    group = A_HEADS // A_KV_HEADS
    scale = HEAD_DIM ** -0.5

    def block(args):
        qb, qib, wib, tb = args
        limit = (tb // CHUNK + 1) * CHUNK
        admissible = key_pos[None, :] < limit[:, None]
        idx_logits = jnp.einsum('bqhd,bsd->bqhs', qib, ki).astype(jnp.float32)
        score = jnp.einsum('bqhs,bqh->bqs', jax.nn.relu(idx_logits), wib.astype(jnp.float32))
        score = jnp.where(admissible[None], score, -jnp.inf)
        _, sel = lax.top_k(score, n_sel)
        valid = sel < limit[None, :, None]
        k_sel = jax.vmap(lambda kk, ii: kk[ii])(k, sel)
        v_sel = jax.vmap(lambda vv, ii: vv[ii])(v, sel)
        qg = qb.reshape(b, Q_BLOCK, A_KV_HEADS, group, HEAD_DIM)
        logits = jnp.einsum('bqngd,bqknd->bqngk', qg, k_sel).astype(jnp.float32) * scale
        logits = jnp.where(valid[:, :, None, None, :], logits, -jnp.inf)
        p = jax.nn.softmax(logits, axis=-1).astype(v.dtype)
        o = jnp.einsum('bqngk,bqknd->bqngd', p, v_sel)
        return o.reshape(b, Q_BLOCK, A_Q)

    o = lax.map(block, (to_blocks(q), to_blocks(qi), to_blocks(wi), t_pos))
    return from_blocks(o) @ w_o

def shared_kv(h, g_kv, w_kv, b_f):
    b, s, _ = h.shape
    k, v, f_logit = jnp.split(rms_norm(h, g_kv) @ w_kv, [B_QK, 2 * B_QK], axis=-1)
    log_f = jax.nn.log_sigmoid((f_logit + b_f).astype(jnp.float32))
    cum = jnp.moveaxis(jnp.cumsum(log_f, axis=1), 2, 1)
    return (k.reshape(b, s, B_HEADS, HEAD_DIM), v.reshape(b, s, B_HEADS, HEAD_DIM), cum)

def fox_attention(xn, w_q, w_o, k, v, cum):
    b, s, _ = xn.shape
    q = (xn @ w_q).reshape(b, s, B_HEADS, HEAD_DIM)
    key_pos = jnp.arange(s)
    t_pos = key_pos.reshape(s // Q_BLOCK, Q_BLOCK)
    cum_q = to_blocks(jnp.moveaxis(cum, 1, 2))
    scale = HEAD_DIM ** -0.5

    def block(args):
        qb, cqb, tb = args
        logits = jnp.einsum('bqhd,bshd->bhqs', qb, k).astype(jnp.float32) * scale
        decay = jnp.moveaxis(cqb, 1, 2)[..., None] - cum[:, :, None, :]
        causal = key_pos[None, :] <= tb[:, None]
        logits = jnp.where(causal[None, None], logits + decay, -jnp.inf)
        p = jax.nn.softmax(logits, axis=-1).astype(v.dtype)
        o = jnp.einsum('bhqs,bshd->bqhd', p, v)
        return o.reshape(b, Q_BLOCK, B_QK)

    o = lax.map(block, (to_blocks(q), cum_q, t_pos))
    return from_blocks(o) @ w_o

def sq_relu_mlp(xn, w_up, w_down):
    return jnp.square(jax.nn.relu(xn @ w_up)) @ w_down

def first_inputs(seed: int = 0) -> dict:
    key = jax.random.key(seed)
    ks = jax.random.split(key, 16)
    f32 = jnp.float32

    def w(k, shape, fan_in):
        return jax.random.normal(k, shape, f32) * (fan_in ** -0.5)

    def gain(k, shape):
        return 1.0 + 0.01 * jax.random.normal(k, shape, f32)

    return {
        "x": jax.random.normal(ks[0], (BATCH, SEQ, D_MODEL), f32),
        "g_attn_a": gain(ks[1], (N_A, D_MODEL)),
        "w_in_a": w(ks[2], (N_A, D_MODEL, A_IN), D_MODEL),
        "w_o_a": w(ks[3], (N_A, A_Q, D_MODEL), A_Q),
        "g_kv": gain(ks[4], (D_MODEL,)),
        "w_kv_b": w(ks[5], (D_MODEL, B_KV_IN), D_MODEL),
        "b_f": jax.random.uniform(ks[6], (B_HEADS,), f32, minval=1.0, maxval=5.0),
        "g_attn_b": gain(ks[7], (N_B, D_MODEL)),
        "w_q_b": w(ks[8], (N_B, D_MODEL, B_QK), D_MODEL),
        "w_o_b": w(ks[9], (N_B, B_QK, D_MODEL), B_QK),
        "g_mlp": gain(ks[10], (DEPTH, D_MODEL)),
        "w_up": w(ks[11], (DEPTH, D_MODEL, D_FF), D_MODEL),
        "w_down": w(ks[12], (DEPTH, D_FF, D_MODEL), D_FF),
        "g_final": gain(ks[13], (D_MODEL,)),
    }

def first_block(x, g_attn_a, w_in_a, w_o_a, g_kv, w_kv_b, b_f, g_attn_b, w_q_b, w_o_b,
              g_mlp, w_up, w_down, g_final):
    h = x
    k_sh = v_sh = cum_sh = None
    for layer in range(DEPTH):
        if layer < N_A:
            h = h + dsa_attention(rms_norm(h, g_attn_a[layer]), w_in_a[layer], w_o_a[layer])
        else:
            if layer == N_A:
                k_sh, v_sh, cum_sh = shared_kv(h, g_kv, w_kv_b, b_f)
            j = layer - N_A
            h = h + fox_attention(rms_norm(h, g_attn_b[j]), w_q_b[j], w_o_b[j], k_sh, v_sh, cum_sh)
        h = h + sq_relu_mlp(rms_norm(h, g_mlp[layer]), w_up[layer], w_down[layer])
    return rms_norm(h, g_final)


N_MIXERS = 2
N_ATTN_LAYERS = (DEPTH + N_MIXERS - 1) // N_MIXERS
N_GMLP_LAYERS = DEPTH // N_MIXERS
N_HEADS = D_MODEL // HEAD_DIM
N_KV_HEADS = N_HEADS // 4
KV_GROUP = N_HEADS // N_KV_HEADS
Q_WIDTH = N_HEADS * HEAD_DIM
KV_WIDTH = N_KV_HEADS * HEAD_DIM
QKV_WIDTH = Q_WIDTH + 2 * KV_WIDTH
ROPE_PAIRS_AXIS = HEAD_DIM // 4
GRID_W = 64
GMLP_FFN = 6 * D_MODEL
GMLP_HALF = GMLP_FFN // 2
GMLP_CHUNK = 128
GMLP_GROUPS = 16
GMLP_GROUP_WIDTH = GMLP_HALF // GMLP_GROUPS
MLP_HIDDEN = 4 * D_MODEL
N_MOD = 6


def rmsnorm(x, g):
    xf = x.astype(jnp.float32)
    y = xf * lax.rsqrt(jnp.mean(xf * xf, axis=-1, keepdims=True) + EPS)
    return (y * g).astype(x.dtype)

def layernorm(x, g, b):
    xf = x.astype(jnp.float32)
    mu = jnp.mean(xf, axis=-1, keepdims=True)
    xc = xf - mu
    y = xc * lax.rsqrt(jnp.mean(xc * xc, axis=-1, keepdims=True) + EPS)
    return (y * g + b).astype(x.dtype)

def modulate(h, shift, scale):
    return h * (1.0 + scale[:, None, :]) + shift[:, None, :]

def axial_rope_tables(seq_len):
    t = jnp.arange(seq_len, dtype=jnp.int32)
    rows = seq_len // GRID_W
    row = (t // GRID_W - rows // 2).astype(jnp.float32)
    col = (t % GRID_W - GRID_W // 2).astype(jnp.float32)
    inv_freq = ROPE_THETA ** (-jnp.arange(ROPE_PAIRS_AXIS, dtype=jnp.float32) / ROPE_PAIRS_AXIS)
    ang = jnp.concatenate([row[:, None] * inv_freq, col[:, None] * inv_freq], axis=-1)
    return jnp.cos(ang), jnp.sin(ang)

def apply_rope_2(x, cos, sin):
    xp = x.astype(jnp.float32).reshape(*x.shape[:-1], HEAD_DIM // 2, 2)
    x1, x2 = xp[..., 0], xp[..., 1]
    c, s = cos[:, None, :], sin[:, None, :]
    out = jnp.stack([x1 * c - x2 * s, x1 * s + x2 * c], axis=-1)
    return out.reshape(x.shape).astype(x.dtype)

def gqa_attention(h, w_qkv, q_g, k_g, w_o, cos, sin):
    B, T, _ = h.shape
    qkv = h @ w_qkv
    q, k, v = jnp.split(qkv, [Q_WIDTH, Q_WIDTH + KV_WIDTH], axis=-1)
    q = apply_rope_2(rmsnorm(q.reshape(B, T, N_HEADS, HEAD_DIM), q_g), cos, sin)
    k = apply_rope_2(rmsnorm(k.reshape(B, T, N_KV_HEADS, HEAD_DIM), k_g), cos, sin)
    v = v.reshape(B, T, N_KV_HEADS, HEAD_DIM)
    n_blocks = T // Q_BLOCK
    qb = q.reshape(B, n_blocks, Q_BLOCK, N_KV_HEADS, KV_GROUP, HEAD_DIM).transpose(1, 0, 2, 3, 4, 5)
    scale = HEAD_DIM ** -0.5

    def one_block(q_blk):
        s = jnp.einsum('bqkgd,bskd->bkgqs', q_blk, k).astype(jnp.float32) * scale
        p = jax.nn.softmax(s, axis=-1).astype(v.dtype)
        return jnp.einsum('bkgqs,bskd->bqkgd', p, v)

    o = lax.map(one_block, qb)
    o = o.transpose(1, 0, 2, 3, 4, 5).reshape(B, T, Q_WIDTH)
    return o @ w_o

def chunked_gmlp(h, w_in, b_in, ln_g, ln_b, w_s, b_s, w_out):
    B, T, _ = h.shape
    z = jax.nn.gelu(h @ w_in + b_in, approximate=False)
    u, v = jnp.split(z, 2, axis=-1)
    v = layernorm(v, ln_g, ln_b)
    v = v.reshape(B, T // GMLP_CHUNK, GMLP_CHUNK, GMLP_GROUPS, GMLP_GROUP_WIDTH)
    v = jnp.einsum('gpq,bnqgc->bnpgc', w_s, v) + b_s.T[None, None, :, :, None]
    v = v.reshape(B, T, GMLP_HALF)
    return (u * v) @ w_out

def sq_relu_mlp_2(h, w_in, w_out):
    return jnp.square(jax.nn.relu(h @ w_in)) @ w_out

def second_inputs(seed: int = 0) -> dict:
    key = jax.random.key(seed)
    ks = jax.random.split(key, 20)

    def nrm(k, shape, scale):
        return jax.random.normal(k, shape, jnp.float32) * scale

    return {
        "x": nrm(ks[0], (BATCH, SEQ, D_MODEL), 1.0),
        "c": nrm(ks[1], (BATCH, D_MODEL), 1.0),
        "ada_w": nrm(ks[2], (DEPTH, D_MODEL, N_MOD * D_MODEL), 0.5 * D_MODEL ** -0.5),
        "ada_b": nrm(ks[3], (DEPTH, N_MOD * D_MODEL), 0.01),
        "norm1_g": 1.0 + nrm(ks[4], (DEPTH, D_MODEL), 0.05),
        "norm2_g": 1.0 + nrm(ks[5], (DEPTH, D_MODEL), 0.05),
        "attn_w_qkv": nrm(ks[6], (N_ATTN_LAYERS, D_MODEL, QKV_WIDTH), D_MODEL ** -0.5),
        "attn_q_norm_g": 1.0 + nrm(ks[7], (N_ATTN_LAYERS, HEAD_DIM), 0.05),
        "attn_k_norm_g": 1.0 + nrm(ks[8], (N_ATTN_LAYERS, HEAD_DIM), 0.05),
        "attn_w_o": nrm(ks[9], (N_ATTN_LAYERS, Q_WIDTH, D_MODEL), Q_WIDTH ** -0.5),
        "gmlp_w_in": nrm(ks[10], (N_GMLP_LAYERS, D_MODEL, GMLP_FFN), D_MODEL ** -0.5),
        "gmlp_b_in": nrm(ks[11], (N_GMLP_LAYERS, GMLP_FFN), 0.01),
        "gmlp_ln_g": 1.0 + nrm(ks[12], (N_GMLP_LAYERS, GMLP_HALF), 0.05),
        "gmlp_ln_b": nrm(ks[13], (N_GMLP_LAYERS, GMLP_HALF), 0.01),
        "gmlp_w_s": nrm(ks[14], (N_GMLP_LAYERS, GMLP_GROUPS, GMLP_CHUNK, GMLP_CHUNK), GMLP_CHUNK ** -0.5),
        "gmlp_b_s": 1.0 + nrm(ks[15], (N_GMLP_LAYERS, GMLP_GROUPS, GMLP_CHUNK), 0.05),
        "gmlp_w_out": nrm(ks[16], (N_GMLP_LAYERS, GMLP_HALF, D_MODEL), GMLP_HALF ** -0.5),
        "mlp_w_in": nrm(ks[17], (DEPTH, D_MODEL, MLP_HIDDEN), D_MODEL ** -0.5),
        "mlp_w_out": nrm(ks[18], (DEPTH, MLP_HIDDEN, D_MODEL), MLP_HIDDEN ** -0.5),
    }

def second_block(x, c, ada_w, ada_b, norm1_g, norm2_g, attn_w_qkv, attn_q_norm_g,
              attn_k_norm_g, attn_w_o, gmlp_w_in, gmlp_b_in, gmlp_ln_g, gmlp_ln_b,
              gmlp_w_s, gmlp_b_s, gmlp_w_out, mlp_w_in, mlp_w_out):
    cond = jax.nn.silu(c)
    cos, sin = axial_rope_tables(x.shape[1])
    for i in range(DEPTH):
        mod = cond @ ada_w[i] + ada_b[i]
        sh1, sc1, g1, sh2, sc2, g2 = jnp.split(mod, N_MOD, axis=-1)
        h = modulate(rmsnorm(x, norm1_g[i]), sh1, sc1)
        j = i // N_MIXERS
        if i % N_MIXERS == 0:
            y = gqa_attention(h, attn_w_qkv[j], attn_q_norm_g[j], attn_k_norm_g[j],
                              attn_w_o[j], cos, sin)
        else:
            y = chunked_gmlp(h, gmlp_w_in[j], gmlp_b_in[j], gmlp_ln_g[j], gmlp_ln_b[j],
                             gmlp_w_s[j], gmlp_b_s[j], gmlp_w_out[j])
        x = x + g1[:, None, :] * y
        h = modulate(rmsnorm(x, norm2_g[i]), sh2, sc2)
        x = x + g2[:, None, :] * sq_relu_mlp_2(h, mlp_w_in[i], mlp_w_out[i])
    return x


def setup_inputs(seed=0):
    out = dict(first_inputs(seed))
    for name, value in second_inputs(seed + 1).items():
        if name != "x":
            out[name + "_2"] = value
    return out


def reference(
    x, g_attn_a, w_in_a, w_o_a, g_kv, w_kv_b, b_f, g_attn_b, w_q_b, w_o_b, g_mlp, w_up, w_down,
    g_final, c_2, ada_w_2, ada_b_2, norm1_g_2, norm2_g_2, attn_w_qkv_2, attn_q_norm_g_2,
    attn_k_norm_g_2, attn_w_o_2, gmlp_w_in_2, gmlp_b_in_2, gmlp_ln_g_2, gmlp_ln_b_2, gmlp_w_s_2,
    gmlp_b_s_2, gmlp_w_out_2, mlp_w_in_2, mlp_w_out_2,
):
    x = first_block(
        x, g_attn_a, w_in_a, w_o_a, g_kv, w_kv_b, b_f, g_attn_b, w_q_b, w_o_b, g_mlp, w_up,
        w_down, g_final,
    )
    return second_block(
        x, c_2, ada_w_2, ada_b_2, norm1_g_2, norm2_g_2, attn_w_qkv_2, attn_q_norm_g_2,
        attn_k_norm_g_2, attn_w_o_2, gmlp_w_in_2, gmlp_b_in_2, gmlp_ln_g_2, gmlp_ln_b_2,
        gmlp_w_s_2, gmlp_b_s_2, gmlp_w_out_2, mlp_w_in_2, mlp_w_out_2,
    )


_drawn_inputs = setup_inputs


def setup_inputs(seed=0):
    import zlib

    import numpy as np

    out = dict(_drawn_inputs(seed))
    spreads = {}
    factors = {'g_attn_a': 3.299,
     'g_kv': 8.0,
     'g_attn_b': 8.0,
     'g_mlp': 4.682,
     'g_final': 5.289,
     'norm1_g_2': 2.997,
     'attn_q_norm_g_2': 8.0,
     'attn_k_norm_g_2': 8.0,
     'gmlp_b_in_2': 63.414,
     'gmlp_ln_g_2': 40.637,
     'gmlp_ln_b_2': 200.0,
     'gmlp_b_s_2': 43.427,
     'norm2_g_2': 8.0}
    for name, (base, spread) in spreads.items():
        noise = np.random.default_rng([zlib.crc32(name.encode()), seed]).standard_normal(out[name].shape)
        drawn = base * np.exp(spread * noise) if base else spread * noise
        out[name] = __import__('jax').numpy.asarray(drawn.astype(out[name].dtype))
    for name, factor in factors.items():
        out[name] = (out[name] * factor).astype(out[name].dtype)
    return out
```

```python
from contextlib import ExitStack

import numpy as np

import concourse.bass as bass
from concourse import mybir

ALU = mybir.AluOpType
ACT_F = mybir.ActivationFunctionType
F32 = mybir.dt.float32
F32R = mybir.dt.float32r

P = 128
S = 512
D = 1024
NT = S // P
KC = D // P
UC = 256
EPS = 1e-6
BIG = 1e30
USED = -3e38
SHUT = -1e38
STAGE = 99


class Engine:

    def __init__(self, sem):
        self.sem, self.count, self.seen, self.eng = sem, 0, {}, None

    def wait(self, waits):
        for sem, value in flat(waits):
            if self.seen.get(sem.name, 0) < value:
                self.seen[sem.name] = value
                self.eng.wait_ge(sem, value)

    def __call__(self, issue, *waits, inc=True):
        self.wait(waits)
        done = issue(self.eng)
        if not inc:
            return None
        done.then_inc(self.sem, 1)
        self.count += 1
        return (self.sem, self.count)

    def last(self):
        return (self.sem, self.count)


class Loader(Engine):

    def __init__(self):
        self.at, self.seen, self.eng = {}, {}, None

    def load(self, sem, issue, *waits):
        self.wait(waits)
        issue(self.eng).then_inc(sem, 16)
        self.at[sem.name] = self.at.get(sem.name, 0) + 16
        return (sem, self.at[sem.name])


def flat(waits):
    for w in waits:
        if w is None:
            continue
        if isinstance(w, tuple) and len(w) == 2 and isinstance(w[1], int):
            yield w
        else:
            yield from flat(w)


class Buf:

    def __init__(self, ap, free=()):
        self.ap, self.ready, self.free = ap, [], list(free)


class Split:

    def __init__(self, hi, lo, free=()):
        self.hi, self.lo = hi, lo
        self.ready = [[] for _ in range(KC)]
        self.free = list(free)


def program(nc, t, consts, out):
    with ExitStack() as ctx:
        PE, ACT, DVE, POOL = (Engine(ctx.enter_context(nc.semaphore(n))) for n in ("pe", "act", "dve", "pool"))
        SP, ACTQ = Loader(), Loader()
        for engine, issuer in ((PE, nc.tensor), (ACT, nc.scalar), (DVE, nc.vector), (POOL, nc.gpsimd), (SP, nc.sync), (ACTQ, nc.scalar)):
            engine.eng = issuer
        body(nc, ctx, t, consts, out, PE, ACT, DVE, POOL, SP, ACTQ)


def body(nc, ctx, t, consts, out, PE, ACT, DVE, POOL, SP, ACTQ):
    def sem(name):
        return ctx.enter_context(nc.semaphore(name))

    def sb(name, shape, dt=F32, stack=ctx):
        return stack.enter_context(nc.sbuf_tensor(name, shape, dt))

    banks = [Buf(ctx.enter_context(nc.psum_tensor(f"bank{i}", [P, 512], F32))) for i in range(8)]

    HT = sb("HT", [P, KC, S])
    h_ready = [[] for _ in range(KC)]
    X = Split(sb("Xhi", [P, KC, S], F32R), sb("Xlo", [P, KC, S], F32R))
    NRAW, NSP = 2, 2
    raw = [Buf(sb(f"raw{i}", [P, KC, UC])) for i in range(NRAW)]
    raw_sem = [sem(f"raw_in{i}") for i in range(NRAW)]
    whi = [sb(f"whi{i}", [P, KC, UC], F32R) for i in range(NSP)]
    wlo = [sb(f"wlo{i}", [P, KC, UC], F32R) for i in range(NSP)]
    wfree = [[] for _ in range(NSP)]
    tmp = [Buf(sb(f"tmp{i}", [P, S])) for i in range(4)]
    held = [Buf(sb(f"held{i}", [P, S])) for i in range(3)]
    rstd = Buf(sb("rstd", [P, S]))
    rope = [None]
    ident = sb("ident", [P, P])
    ones = sb("ones", [P, P])
    mean = sb("mean", [P, P])
    head_mean = sb("head_mean", [P, P])
    perm = [sb(f"perm{i}", [P, P]) for i in range(2)]
    one_hot = sb("one_hot", [P, 16])
    eps = sb("eps", [P, 1])
    V1 = sb("V1", [P, 114])
    V2 = sb("V2", [P, 96])
    bf = sb("bf", [P, 16])
    cond = sb("cond", [P, 3, KC])
    MOD = [sb(f"MOD{i}", [P, 48]) for i in range(2)]
    GM = sb("GM", [P, 4, KC])
    acc = [Buf(sb(f"acc{i}", [P, UC])) for i in range(2)]
    stats = sb("stats", [P, 6, 4])
    stat = [Buf(stats[:, i, :]) for i in range(6)]
    bst = sb("bst", [P, NT, 6, 6])
    mv = sb("mv", [P, NT, 2])
    rsv = sb("rsv", [P, NT])
    nmr = sb("nmr", [P, NT])

    tmp_at = [0]

    def scratch():
        b = tmp[tmp_at[0] % len(tmp)]
        tmp_at[0] += 1
        return b

    held_at = [0]

    def hold():
        b = held[held_at[0] % len(held)]
        held_at[0] += 1
        return b

    later = []

    def defer(n, fn):
        later.append([n, fn])

    def tick(force=False):
        for item in later:
            item[0] -= 1
        while True:
            due = [item for item in later if force or item[0] <= 0]
            if not due:
                return
            later.remove(due[0])
            due[0][1]()

    s_const = sem("const_in")

    def const(dst, name):
        src = consts[name]
        return SP.load(s_const, lambda e, dst=dst, src=src: e.dma_start(dst, src))

    s_ident = sem("ident_in")
    i_in = SP.load(s_ident, lambda e: e.dma_start(ident[:], consts["ident"]))
    DVE(lambda e: e.memset(mean[:], 1.0 / D))
    DVE(lambda e: e.memset(ones[:], 1.0))
    d_const = DVE(lambda e: e.memset(eps[:], EPS))
    s_vec = sem("vec_in")

    def phase_end():
        return [PE.last(), ACT.last(), DVE.last(), POOL.last()]

    def block_of(w, r0, c0, n):
        return w[r0:r0 + D, c0:c0 + n].rearrange("(c p) n -> p c n", p=P)

    plan = []

    def plan_cols(name, w, c0, n, r0=0):
        for c in range(c0, c0 + n, UC):
            k = min(UC, c0 + n - c)
            plan.append((name, block_of(w, r0, c, k), k))

    ada = [("ada", block_of(t["ada_w_2"][i], 0, c, UC), (i, c // P)) for i in range(2) for c in range(0, 6 * D, UC)]

    def plan_mlp(name, up, down, with_ada):
        start = len(plan)

        def up_g(g):
            plan_cols(name + "u", up, g * D, D)

        def down_g(g):
            plan_cols(name + "d", down, 0, D, r0=g * D)
        for f, g in ((up_g, 0), (up_g, 1), (down_g, 0), (up_g, 2), (down_g, 1), (up_g, 3), (down_g, 2), (down_g, 3)):
            f(g)
        if with_ada:
            units = plan[start:]
            del plan[start:]
            for i, u in enumerate(units):
                plan.append(u)
                if 1 <= i < 25:
                    plan.append(ada.pop(0))

    wa = t["w_in_a"][0]
    plan_cols("qi", wa, 1536, 512)
    plan_cols("ki", wa, 2048, 72)
    plan_cols("qa", wa, 0, 1024)
    plan_cols("ka", wa, 1024, 256)
    plan_cols("va", wa, 1280, 256)
    plan_cols("oa", t["w_o_a"][0], 0, 1024)
    plan_mlp("m0", t["w_up"][0], t["w_down"][0], True)
    wk = t["w_kv_b"]
    plan_cols("fb", wk, 2048, 16)
    plan_cols("kb", wk, 0, 1024)
    plan_cols("vb", wk, 1024, 1024)
    plan_cols("qb", t["w_q_b"][0], 0, 1024)
    plan_cols("ob", t["w_o_b"][0], 0, 1024)
    plan_mlp("m1", t["w_up"][1], t["w_down"][1], True)
    wq = t["attn_w_qkv_2"][0]
    plan_cols("kc", wq, 1024, 256)
    plan_cols("vc", wq, 1280, 256)
    plan_cols("qc", wq, 0, 1024)
    plan_cols("oc", t["attn_w_o_2"][0], 0, 1024)
    plan_mlp("m2", t["mlp_w_in_2"][0], t["mlp_w_out_2"][0], False)
    wg = t["gmlp_w_in_2"][0]
    plan_cols("gv", wg, 3072, 3072)
    for g in range(3):
        plan_cols("gu", wg, g * D, D)
        plan_cols("go", t["gmlp_w_out_2"][0], 0, D, r0=g * D)
    plan_mlp("m3", t["mlp_w_in_2"][1], t["mlp_w_out_2"][1], False)

    loaded, split_at, used = [0], [0], [0]
    loads, splits = {}, {}
    mod_ready = [[], []]
    v2_ready = []
    cond_ready = []

    def load_next():
        n = loaded[0]
        if n >= len(plan):
            return
        name, src, k = plan[n]
        k = UC if name == "ada" else k
        place = raw[n % NRAW]
        loads[n] = SP.load(raw_sem[n % NRAW], lambda e, place=place, src=src, k=k: e.dma_start(place.ap[:, :, 0:k], src), place.free)
        place.free = []
        loaded[0] += 1

    gemm_no = [0]

    def split_next():
        while split_at[0] < len(plan):
            n = split_at[0]
            split_at[0] += 1
            if n >= loaded[0]:
                load_next()
            name, _, k = plan[n]
            place = raw[n % NRAW]
            if name == "ada":
                ada_unit(place, loads[n], *k)
                load_next()
                continue
            slot = gemm_no[0] % NSP
            gemm_no[0] += 1
            hi, lo = whi[slot], wlo[slot]
            ready = []
            for c0, c1 in ((0, KC // 2), (KC // 2, KC)):
                a = ACT(lambda e: e.activation(hi[:, c0:c1, 0:k], place.ap[:, c0:c1, 0:k], ACT_F.Copy), loads[n], wfree[slot])
                p = POOL(lambda e: e.tensor_tensor(
                    lo[:, c0:c1, 0:k], place.ap[:, c0:c1, 0:k], hi[:, c0:c1, 0:k].bitcast(F32), ALU.subtract), a, wfree[slot])
                ready += [[a, p]] * (KC // 2)
            place.free = [p]
            splits[n] = (name, slot, ready)
            load_next()
            return

    def ada_unit(place, arrived, layer, col):
        a = acc[(col // 2) % 2]
        cd = cond[:, 2, :]
        tok = DVE(lambda e: e.tensor_scalar(a.ap[:], place.ap[:, 0, :], cd[:, 0:1], None, ALU.mult), arrived, cond_ready, a.free)
        for c in range(1, KC):
            tok = DVE(lambda e, c=c: e.scalar_tensor_tensor(a.ap[:], place.ap[:, c, :], cd[:, c:c + 1], a.ap[:], ALU.mult, ALU.add), tok)
        place.free = [tok]
        a.ready = [tok]

        def sums():
            b = banks[7]
            for j in range(2):
                m = PE(lambda e, j=j: e.matmul(b.ap[:, j:j + 1], a.ap[:, j * P:(j + 1) * P], ones[:, 0:1], start=True, stop=True),
                       a.ready, b.free)
            a.free = [m]
            d = DVE(lambda e: e.tensor_tensor(MOD[layer][:, col:col + 2], b.ap[:, 0:2],
                                              V2[:, layer * 48 + col:layer * 48 + col + 2], ALU.add), m, v2_ready)
            b.free = [d]
            mod_ready[layer] = [d]
        defer(3, sums)

    current = []

    def unit(name):
        while used[0] not in splits:
            if plan[used[0]][0] == "ada" and used[0] < split_at[0]:
                used[0] += 1
                continue
            split_next()
        n = used[0]
        used[0] += 1
        got, slot, ready = splits.pop(n)
        assert got == name, (got, name)
        return slot, ready

    gb = [0]

    def gemm_bank():
        b = banks[gb[0] % 4]
        gb[0] += 1
        return b

    def gemm_fm(name, x, n_cols, evac):
        at = 0
        while at < n_cols:
            slot, ready = unit(name)
            split_next()
            k = min(UC, n_cols - at)
            for j in range(0, k, P):
                m_cols = min(P, k - j)
                b = gemm_bank()
                n = 0
                for c in range(KC):
                    for w, v in ((whi, x.hi), (whi, x.lo), (wlo, x.hi)):
                        m = PE(lambda e, w=w, v=v, c=c, j=j, n=n, b=b, m_cols=m_cols: e.matmul(
                            b.ap[0:m_cols, :], w[slot][:, c, j:j + m_cols], v[:, c, :], start=(n == 0), stop=(n == 3 * KC - 1)),
                            ready[c], b.free, x.ready[c], inc=(n == 3 * KC - 1))
                        n += 1
                x.free = [m]
                wfree[slot] = [m]
                tick()
                evac((at + j) // P, b, m)
            at += k

    def gemm_tm(name, x, n_cols, evac):
        at = 0
        while at < n_cols:
            slot, ready = unit(name)
            split_next()
            k = min(UC, n_cols - at)
            for i in range(NT):
                b = gemm_bank()
                n = 0
                for c in range(KC):
                    for v, w in ((x.hi, whi), (x.hi, wlo), (x.lo, whi)):
                        m = PE(lambda e, w=w, v=v, c=c, i=i, n=n, b=b, k=k: e.matmul(
                            b.ap[:, 0:k], v[:, c, i * P:(i + 1) * P], w[slot][:, c, 0:k], start=(n == 0), stop=(n == 3 * KC - 1)),
                            ready[c], b.free, x.ready[c], inc=(n == 3 * KC - 1))
                        n += 1
                x.free = [m]
                wfree[slot] = [m]
                tick()
                evac(i, at, k, b, m)
            at += k

    def to_split(full, ready, x, c):
        a = ACT(lambda e: e.activation(x.hi[:, c, :], full, ACT_F.Copy), ready, x.free)
        d = (POOL if c % 3 == 1 else DVE)(lambda e: e.tensor_tensor(x.lo[:, c, :], full, x.hi[:, c, :].bitcast(F32), ALU.subtract), a)
        x.ready[c] = [a, d]
        return d

    def square(c):
        b, q = banks[6], hold()
        a = ACT(lambda e: e.activation(q.ap[:], HT[:, c, :], ACT_F.Square), h_ready[c], q.free)

        def add():
            q.free = [PE(lambda e: e.matmul(b.ap[:], mean[:], q.ap[:], start=(c == 0), stop=(c == KC - 1)), a, b.free, d_const)]
        defer(1, add)

    def mean_square():
        tick(force=True)
        b, m = banks[6], PE.last()
        a = ACT(lambda e: e.activation(rstd.ap[:], b.ap[:], ACT_F.Sqrt, bias=eps[:, 0:1]), m, rstd.free)
        b.free = [a]
        d = DVE(lambda e: e.reciprocal(rstd.ap[:], rstd.ap[:]), a)
        rstd.ready = [d]

    def normed(x, gain, shift, ready):
        for c in range(KC):
            q = scratch()
            d = DVE(lambda e, q=q, c=c: e.scalar_tensor_tensor(q.ap[:], HT[:, c, :], gain[:, c:c + 1], rstd.ap[:], ALU.mult, ALU.mult),
                    rstd.ready, ready, q.free)
            if shift is not None:
                d = DVE(lambda e, q=q, c=c: e.tensor_scalar(q.ap[:], q.ap[:], shift[:, c:c + 1], None, ALU.add), d)
            rstd.free = [d]
            q.free = [to_split(q.ap[:], d, x, c)]

    def add_to_h(o, b, m, gate=None, ready=(), last=True):
        if gate is None:
            d = DVE(lambda e: e.tensor_tensor(HT[:, o, :], b.ap[:], HT[:, o, :], ALU.add), m, h_ready[o])
        else:
            d = DVE(lambda e: e.scalar_tensor_tensor(HT[:, o, :], b.ap[:], gate[:, o:o + 1], HT[:, o, :], ALU.mult, ALU.add), m, h_ready[o], ready)
        b.free = [d]
        h_ready[o] = [d]
        if last:
            square(o)

    def mlp(name, gate=None, ready=()):
        with ExitStack() as region:
            free = phase_end()
            H = [Split(sb(f"{name}Hhi{i}", [P, KC, S], F32R, region), sb(f"{name}Hlo{i}", [P, KC, S], F32R, region), free) for i in range(2)]

            def up(g):
                h = H[g % 2]
                write_after = list(h.free)

                def evac(o, b, m):
                    q, r = scratch(), scratch()
                    a = ACT(lambda e: e.activation(q.ap[:], b.ap[:], ACT_F.Relu), m, q.free)
                    b.free = [a]
                    a2 = ACT(lambda e: e.activation(h.hi[:, o, :], q.ap[:], ACT_F.Square), a, write_after)
                    d = DVE(lambda e: e.tensor_tensor(r.ap[:], q.ap[:], q.ap[:], ALU.mult), a, r.free)
                    q.free = [a2, d]
                    d = DVE(lambda e: e.tensor_tensor(h.lo[:, o, :], r.ap[:], h.hi[:, o, :].bitcast(F32), ALU.subtract), a2, d, write_after)
                    r.free = [d]
                    h.ready[o] = [a2, d]
                gemm_fm(name + "u", X, D, evac)

            def down(g):
                gemm_fm(name + "d", H[g % 2], D, lambda o, b, m: add_to_h(o, b, m, gate, ready, g == 3 and name != "m3"))
            for f, g in ((up, 0), (up, 1), (down, 0), (up, 2), (down, 1), (up, 3), (down, 2), (down, 3)):
                f(g)

    rb = [0]

    def rotate(src, ready, p, rows, done):
        b, CS = banks[4], rope[0]
        rb[0] += 1
        m = PE(lambda e: e.matmul(b.ap[0:rows, :], perm[p][0:rows, 0:rows], src.ap[0:rows, :], start=True, stop=True), ready, b.free, c_ready)
        r = scratch()
        d = DVE(lambda e: e.tensor_tensor(r.ap[0:rows, :], b.ap[0:rows, :], CS.ap[0:rows, 1, :], ALU.mult), m, r.free, CS.ready)
        b.free = [d]
        q = POOL(lambda e: e.tensor_tensor(src.ap[0:rows, :], src.ap[0:rows, :], CS.ap[0:rows, 0, :], ALU.mult), m, ready, CS.ready)
        d = done(src, r, [d, q])
        src.free, r.free = [d], [d]

    def add_into(dst, ready_list, on=None):
        def done(x1, x2, ready):
            d = (on or DVE)(lambda e: e.tensor_tensor(dst, x1.ap[:], x2.ap[:], ALU.add), ready)
            ready_list.append(d)
            return d
        return done

    def add_twice(dsts, ready_list):
        def done(x1, x2, ready):
            for i, dst in enumerate(dsts):
                for half in range(2):
                    d = DVE(lambda e, i=i, half=half, dst=dst: e.tensor_tensor(
                        dst[64 * half:64 * half + 64, :], x1.ap[64 * i:64 * i + 64, :], x2.ap[64 * i:64 * i + 64, :], ALU.add), ready)
            ready_list.append(d)
            return d
        return done

    def copy_out(b, m, rows=P):
        q = hold()
        a = ACT(lambda e: e.activation(q.ap[0:rows, :], b.ap[0:rows, :], ACT_F.Copy), m, q.free)
        b.free = [a]
        return q, a

    def attention(heads_q, heads_k, heads_v, mask, width, extra, ready, x, PB, PT):
        scale = 0.125
        steps = [(h, i) for h in range(16) for i in range(NT)]
        prob = {}
        write_after = list(x.free)

        def scores(n):
            h, i = steps[n]
            w = width(i)
            b, pb, st = banks[n % 3], PB[n % len(PB)], stat[n % len(stat)]
            q, k = heads_q(h, i), heads_k(h, w)
            e2 = extra(h, i, w) if extra else None
            m = PE(lambda e: e.matmul(b.ap[:, 0:w], q, k, start=True, stop=e2 is None), ready, b.free)
            if e2:
                l2, r2, tok = e2
                m = PE(lambda e: e.matmul(b.ap[:, 0:w], l2, r2, start=False, stop=True), tok)
                extra_free(h, m)
            mk = mask(i, w) if mask else None
            if mk is not None:
                d = DVE(lambda e: e.tensor_tensor_reduce(pb.ap[:, 0:w], b.ap[:, 0:w], mk, -scale, 3e38, ALU.add, ALU.min, st.ap[:, 0:1]),
                        m, pb.free, st.free)
            else:
                d = DVE(lambda e: e.tensor_scalar(pb.ap[:, 0:w], b.ap[:, 0:w], -scale, None, ALU.mult, ALU.min, accum_out=st.ap[:, 0:1]),
                        m, pb.free, st.free)
            b.free = [d]
            a = ACT(lambda e: e.activation(pb.ap[:, 0:w], pb.ap[:, 0:w], ACT_F.Exp, bias=st.ap[:, 0:1], scale=-1.0, accum_out=st.ap[:, 1:2]), d)
            d = DVE(lambda e: e.reciprocal(st.ap[:, 2:3], st.ap[:, 1:2]), a)
            g = DVE(lambda e: e.tensor_scalar(pb.ap[:, 0:w], pb.ap[:, 0:w], st.ap[:, 2:3], None, ALU.mult), d)
            st.free = [g]
            prob[n] = g

        def turn(n):
            h, i = steps[n]
            w = width(i)
            b, pb, pt = banks[(3, 4, 7)[n % 3]], PB[n % len(PB)], PT[h % 2]
            for j in range(0, w, P):
                m = PE(lambda e, j=j: e.transpose(b.ap[:, j:j + P], pb.ap[:, j:j + P], ident[:]), prob[n], b.free)
            pb.free = [m]
            dst = pt.ap[:, 0:w // P, i * P:(i + 1) * P]
            src = b.ap[:, 0:w].rearrange("p (j q) -> p j q", q=P)
            if n % 2:
                v = ACT(lambda e: e.activation(dst, src, ACT_F.Copy), m, pt.free)
            else:
                v = DVE(lambda e: e.tensor_copy(dst, src), m, pt.free)
            b.free = [v]
            if i == 0:
                pt.ready = []
            pt.ready.append(v)

        def values(h):
            b, pt = banks[5 + (h // 2) % 2], PT[h % 2]
            o = 64 * (h % 2)
            full = width(0) == S
            for j in range(NT):
                q0 = 0 if full else j * P
                v = heads_v(h, j)
                m = PE(lambda e, j=j, q0=q0, v=v: e.matmul(b.ap[o:o + 64, q0:S], v, pt.ap[:, j, q0:S], start=(j == 0), stop=(j == NT - 1)),
                       pt.ready, b.free)
            pt.free = [m]
            if h % 2:
                c = h // 2
                a = ACT(lambda e: e.activation(x.hi[:, c, :], b.ap[:], ACT_F.Copy), m, write_after)
                d = DVE(lambda e: e.tensor_tensor(x.lo[:, c, :], b.ap[:], x.hi[:, c, :].bitcast(F32), ALU.subtract), a)
                b.free = [d]
                x.ready[c] = [a, d]

        LAG = 4
        for n in range(len(steps) + LAG + 3):
            if LAG <= n < len(steps) + LAG:
                turn(n - LAG)
            if n < len(steps):
                scores(n)
            if n >= LAG + 5 - 1 and (n - LAG - 4) % NT == 0:
                values((n - LAG - 4) // NT)
        values(15)

    extra_hook = [None]

    def extra_free(h, m):
        extra_hook[0](h, m)

    with ExitStack() as region:
        XT = sb("XT", [P, NT, D], F32, region)
        R1 = sb("R1", [114, P], F32, region)
        R2 = sb("R2", [96, P], F32, region)
        s_x = [sem(f"x_in{i}") for i in range(NT)]
        xin = [SP.load(s_x[i], lambda e, i=i: e.dma_start(XT[:, i, :], t["x"][0, i * P:(i + 1) * P, :])) for i in range(NT)]
        row = 0
        VEC = {}
        for name, src, n in (
            ("g_attn_a", t["g_attn_a"][0], 8), ("g_kv", t["g_kv"], 8), ("g_attn_b", t["g_attn_b"][0], 8),
            ("g_mlp0", t["g_mlp"][0], 8), ("g_mlp1", t["g_mlp"][1], 8), ("g_final", t["g_final"], 8),
            ("n1_0", t["norm1_g_2"][0], 8), ("n1_1", t["norm1_g_2"][1], 8), ("n2_0", t["norm2_g_2"][0], 8),
            ("n2_1", t["norm2_g_2"][1], 8), ("c", t["c_2"][0], 8), ("b_in", t["gmlp_b_in_2"][0, 0:3072], 24),
        ):
            v = ACTQ.load(s_vec, lambda e, row=row, n=n, src=src: e.dma_start(R1[row:row + n, :], src.rearrange("(r k) -> r k", k=P)))
            VEC[name] = V1[:, row:row + n]
            row += n
        for name, src in (("qg", t["attn_q_norm_g_2"]), ("kg", t["attn_k_norm_g_2"])):
            for half in range(2):
                v = ACTQ.load(s_vec, lambda e, row=row, half=half, src=src: e.dma_start(R1[row:row + 1, 64 * half:64 * half + 64], src))
            VEC[name] = V1[:, row:row + 1]
            row += 1
        for i in range(2):
            v = ACTQ.load(s_vec, lambda e, i=i: e.dma_start(R2[48 * i:48 * i + 48, :], t["ada_b_2"][i].rearrange("(r k) -> r k", k=P)))
        vec_in = ACTQ.load(s_vec, lambda e: e.dma_start(bf[:], t["b_f"].partition_broadcast(P)))
        for _ in range(NRAW):
            load_next()
        const(head_mean[:], "head_mean")
        const(perm[0][:], "perm_half")
        const(perm[1][:], "perm_pair")
        c_ready = const(one_hot[:], "one_hot")
        for c in range(KC):
            b = gemm_bank()
            for i in range(NT):
                m = PE(lambda e, i=i, c=c, b=b: e.transpose(b.ap[:, i * P:(i + 1) * P], XT[:, i, c * P:(c + 1) * P], ident[:]), xin[i], i_in, b.free)
            if c % 2:
                v = DVE(lambda e, c=c, b=b: e.tensor_copy(HT[:, c, :], b.ap[:]), m)
            else:
                v = ACT(lambda e, c=c, b=b: e.activation(HT[:, c, :], b.ap[:], ACT_F.Copy), m)
            b.free = [v]
            h_ready[c] = [v]
            tick()
            square(c)
        split_next()
        b = banks[4]
        m = PE(lambda e: e.transpose(b.ap[:, 0:114], R1[:], ident[0:114, 0:114]), vec_in)
        d = DVE(lambda e: e.tensor_copy(V1[:], b.ap[:, 0:114]), m)
        b.free = [d]
        v1_ready = [d]
        b = banks[5]
        m = PE(lambda e: e.transpose(b.ap[:, 0:96], R2[:], ident[0:96, 0:96]), vec_in)
        d = DVE(lambda e: e.tensor_copy(V2[:], b.ap[:, 0:96]), m)
        b.free = [d]
        v2_ready.append(d)
        mean_square()
        normed(X, VEC["g_attn_a"], None, [v1_ready, h_ready])
        a = ACT(lambda e: e.activation(cond[:, 0, :], VEC["c"], ACT_F.Exp, scale=-1.0), v1_ready)
        d = DVE(lambda e: e.tensor_scalar(cond[:, 0, :], cond[:, 0, :], 1.0, None, ALU.add), a)
        d = DVE(lambda e: e.reciprocal(cond[:, 1, :], cond[:, 0, :]), d)
        d = DVE(lambda e: e.tensor_tensor(cond[:, 2, :], cond[:, 1, :], VEC["c"], ALU.mult), d)
        cond_ready.append(d)

    s_rope = sem("rope_in")
    with ExitStack() as region:
        free = phase_end()
        Q = sb("QA", [P, KC, S], F32, region)
        K2 = [sb(f"KA{i}", [P, S], F32, region) for i in range(4)]
        V = sb("VA", [P, NT, 256], F32, region)
        PB = [Buf(sb(f"PA{i}", [P, S], F32, region), free) for i in range(5)]
        PT = [Buf(sb(f"PTA{i}", [P, NT, S], F32, region), free) for i in range(2)]
        QI = sb("QI", [P, 4, S], F32, region)
        KI = sb("KI", [P, S], F32, region)
        WI = sb("WI", [P, NT, 8], F32, region)
        SC = [Buf(sb(f"SC{i}", [P, S], F32, region), free) for i in range(3)]
        SC2 = Buf(sb("SCW", [P, S], F32, region), free)
        top = Buf(sb("top", [P, 8], F32, region), free)
        M = [sb(f"MA{i}", [P, (i + 1) * P], F32, region) for i in range(NT)]
        rope[0] = Buf(sb("rope_a", [P, 2, S], F32, region))
        rope[0].ready = [SP.load(s_rope, lambda e: e.dma_start(rope[0].ap[:], consts["rope_a"]))]
        i_ready, a_ready = [free], []
        DVE(lambda e: e.memset(M[0][:], 0.0), free)
        mask_ready = [DVE(lambda e: e.memset(M[0][0:64, 64:128], -BIG), DVE.last())]

        def evac_qi(o, b, m):
            q, a = copy_out(b, m)
            defer(1, lambda: rotate(q, a, 0, P, add_into(QI[:, o, :], i_ready)))
        DVE(lambda e: e.memset(top.ap[:], 0.0), free)
        gemm_fm("qi", X, 512, evac_qi)

        def evac_ki(o, b, m):
            q, a = copy_out(b, m, 72)
            bw = banks[6]

            def finish():
                for i in range(NT):
                    mt = PE(lambda e, i=i: e.transpose(bw.ap[:, 8 * i:8 * i + 8], q.ap[64:72, i * P:(i + 1) * P], ident[64:72, 64:72]), a, bw.free)
                w = DVE(lambda e: e.tensor_scalar(WI[:], bw.ap[:, 0:32].rearrange("p (i h) -> p i h", h=8),
                                                  8 ** -0.5 * 64 ** -0.5, None, ALU.mult), mt)
                bw.free = [w]
                i_ready.append(w)
                rotate(q, [a, mt], 0, 64, lambda x1, x2, rdy: ki_add(x1, x2, rdy))

            def ki_add(x1, x2, rdy):
                for half in range(2):
                    d = DVE(lambda e, half=half: e.tensor_tensor(KI[64 * half:64 * half + 64, :], x1.ap[0:64, :], x2.ap[0:64, :], ALU.add), rdy)
                i_ready.append(d)
                return d
            defer(1, finish)
        gemm_fm("ki", X, 72, evac_ki)

        def evac_qa(o, b, m):
            q, a = copy_out(b, m)
            defer(1, lambda: rotate(q, a, 0, P, add_into(Q[:, o, :], a_ready, POOL)))
            select_some(9)

        def select():
            for i in range(1, NT):
                w = (i + 1) * P
                s = SC[i - 1]
                for h in range(8):
                    b = banks[5 + h % 3]
                    o = 64 * (h % 2)
                    m = PE(lambda e, h=h, o=o, i=i, w=w: e.matmul(b.ap[:, 0:w], QI[o:o + 64, h // 2, i * P:(i + 1) * P], KI[o:o + 64, 0:w],
                                                         start=True, stop=True), i_ready, b.free)
                    q = scratch()
                    a = ACT(lambda e, q=q, w=w: e.activation(q.ap[:, 0:w], b.ap[:, 0:w], ACT_F.Relu), m, q.free)
                    b.free = [a]
                    if h == 0:
                        d = DVE(lambda e, q=q, i=i, h=h, w=w, s=s: e.tensor_scalar(s.ap[:, 0:w], q.ap[:, 0:w], WI[:, i, h:h + 1], None, ALU.mult), a, s.free)
                    else:
                        d = DVE(lambda e, q=q, i=i, h=h, w=w, s=s: e.scalar_tensor_tensor(
                            s.ap[:, 0:w], q.ap[:, 0:w], WI[:, i, h:h + 1], s.ap[:, 0:w], ALU.mult, ALU.add), a, d)
                    q.free = [d]
                    yield
                d = DVE(lambda e, s=s, w=w: e.memset(s.ap[0:64, w - 64:w], SHUT), d)
                x1, x2 = s, SC2
                for _ in range(16):
                    d = DVE(lambda e, x1=x1, w=w: e.max(top.ap[:], x1.ap[:, 0:w]), d)
                    d = DVE(lambda e, x1=x1, x2=x2, w=w: e.match_replace(x2.ap[:, 0:w], top.ap[:], x1.ap[:, 0:w], USED), d)
                    x1, x2 = x2, x1
                    yield
                    yield
                d = DVE(lambda e, i=i, w=w, x1=x1: e.tensor_scalar(M[i][:], x1.ap[:, 0:w], USED, -BIG, ALU.not_equal, ALU.mult), d, free)
                mask_ready[:] = [d]
                yield

        selecting = [None]

        def select_some(n):
            if selecting[0] is None:
                selecting[0] = select()
            for _ in range(n):
                next(selecting[0], None)
        gemm_fm("qa", X, 1024, evac_qa)

        def evac_ka(o, b, m):
            q, a = copy_out(b, m)
            defer(1, lambda: rotate(q, a, 0, P, add_twice([K2[2 * o], K2[2 * o + 1]], a_ready)))
            select_some(9)
        gemm_fm("ka", X, 256, evac_ka)

        def evac_va(i, at, k, b, m):
            a = ACT(lambda e: e.activation(V[:, i, at:at + k], b.ap[:, 0:k], ACT_F.Copy), m, free)
            b.free = [a]
            a_ready.append(a)
            select_some(5)
        gemm_tm("va", X, 256, evac_va)
        tick(force=True)
        select_some(1000)
        attention(
            lambda h, i: Q[64 * (h % 2):64 * (h % 2) + 64, h // 2, i * P:(i + 1) * P],
            lambda h, w: K2[h // 4][64 * (h % 2):64 * (h % 2) + 64, 0:w],
            lambda h, j: V[:, j, 64 * (h // 4):64 * (h // 4) + 64],
            lambda i, w: M[i][:, 0:w], lambda i: (i + 1) * P, None, [a_ready, mask_ready], X, PB, PT)
        gemm_fm("oa", X, 1024, lambda o, b, m: add_to_h(o, b, m))
        tick(force=True)
        end_of_a = phase_end()

    if STAGE >= 2:
        mean_square()
        normed(X, VEC["g_mlp0"], None, [v1_ready, h_ready])
        mlp("m0")
        tick(force=True)

    if STAGE >= 3:
        with ExitStack() as region:
            mean_square()
            free = phase_end()
            Q = sb("QB", [P, KC, S], F32, region)
            K = sb("KB", [P, KC, S], F32, region)
            V = sb("VB", [P, NT, D], F32, region)
            PB = [Buf(sb(f"PBB{i}", [P, S], F32, region), free) for i in range(5)]
            PT = [Buf(sb(f"PTB{i}", [P, NT, S], F32, region), free) for i in range(2)]
            tsum = sb("tsum", [P, S], F32, region)
            LF = sb("LF", [P, 4, NT * 16], F32, region)
            CK = sb("CK", [P, S], F32, region)
            CQ = sb("CQ", [P, S], F32, region)
            MH = [Buf(sb(f"MH{i}", [P, S], F32, region), free) for i in range(2)]
            s_tsum = sem("tsum_in")
            tri = sb("tri", [P, S], F32, region)
            SP.load(s_tsum, lambda e: e.dma_start(tri[:], consts["tri"]), end_of_a)
            tsum_in = SP.load(s_tsum, lambda e: e.dma_start(tsum[:], consts["tsum"]), end_of_a)
            DVE(lambda e: e.memset(CK[:], 0.0), free)
            for o in (32, 96):
                DVE(lambda e: e.memset(CK[o:o + 16, :], 1.0), DVE.last())
            DVE(lambda e: e.memset(CQ[:], 0.0), free)
            for o in (0, 64):
                c_set = DVE(lambda e: e.memset(CQ[o:o + 16, :], 1.0), DVE.last())
            normed(X, VEC["g_kv"], None, [v1_ready, h_ready])
            f_ready, b_ready = [], [free]

            def evac_f(i, at, k, b, m):
                d = DVE(lambda e: e.tensor_tensor(LF[:, 0, 16 * i:16 * i + 16], b.ap[:, 0:16], bf[:], ALU.add), m, free)
                b.free = [d]
                f_ready.append(d)
            gemm_tm("fb", X, 16, evac_f)
            d0 = DVE(lambda e: e.tensor_scalar(LF[:, 1, :], LF[:, 0, :], 0.0, None, ALU.min), f_ready)
            a = ACT(lambda e: e.activation(LF[:, 2, :], LF[:, 0, :], ACT_F.Abs), f_ready)
            a = ACT(lambda e: e.activation(LF[:, 3, :], LF[:, 2, :], ACT_F.Exp, scale=-1.0), a)
            d = DVE(lambda e: e.tensor_scalar(LF[:, 2, :], LF[:, 3, :], 1.0, None, ALU.add), a)
            a = ACT(lambda e: e.activation(LF[:, 3, :], LF[:, 2, :], ACT_F.Ln), d)
            d_lf = DVE(lambda e: e.tensor_tensor(LF[:, 0, :], LF[:, 1, :], LF[:, 3, :], ALU.subtract), a, d0)

            def running_sum():
                b = banks[6]
                for i in range(NT):
                    m = PE(lambda e, i=i: e.matmul(b.ap[0:16, P * i:S], LF[:, 0, 16 * i:16 * i + 16], tsum[:, 0:S - P * i],
                                                   start=(i == 0), stop=(i == NT - 1)), d_lf, tsum_in, b.free)
                for o in (32, 96):
                    a = ACT(lambda e: e.activation(CQ[o:o + 16, :], b.ap[0:16, :], ACT_F.Copy, scale=8.0), m, c_set)
                for o in (0, 64):
                    d = DVE(lambda e: e.tensor_scalar(CK[o:o + 16, :], b.ap[0:16, :], -8.0, None, ALU.mult), m, a)
                b.free = [d]
                b_ready.extend([a, d])
            defer(1, running_sum)

            def keep(dst):
                def evac(o, b, m):
                    a = ACT(lambda e: e.activation(dst[:, o, :], b.ap[:], ACT_F.Copy), m, free)
                    b.free = [a]
                    b_ready.append(a)
                return evac
            gemm_fm("kb", X, 1024, keep(K))

            def evac_vb(i, at, k, b, m):
                a = ACT(lambda e: e.activation(V[:, i, at:at + k], b.ap[:, 0:k], ACT_F.Copy), m, free)
                b.free = [a]
                b_ready.append(a)
            gemm_tm("vb", X, 1024, evac_vb)
            normed(X, VEC["g_attn_b"], None, [v1_ready, h_ready])
            gemm_fm("qb", X, 1024, keep(Q))
            tick(force=True)

            def decay(h, i, w):
                mh, o = MH[h % 2], 64 * (h % 2)
                if i == 0:
                    g = POOL(lambda e: e.tensor_scalar(mh.ap[:], CK[:], one_hot[:, h:h + 1], None, ALU.mult), b_ready, mh.free, c_ready)
                    mh.ready = [g]
                    mh.free = []
                return CQ[o:o + 48, i * P:(i + 1) * P], mh.ap[o:o + 48, 0:w], mh.ready

            def used_decay(h, m):
                MH[h % 2].free = [m]
            extra_hook[0] = used_decay
            attention(
                lambda h, i: Q[64 * (h % 2):64 * (h % 2) + 64, h // 2, i * P:(i + 1) * P],
                lambda h, w: K[64 * (h % 2):64 * (h % 2) + 64, h // 2, 0:w],
                lambda h, j: V[:, j, 64 * h:64 * h + 64],
                lambda i, w: tri[:, 384 - i * P:384 - i * P + w], lambda i: (i + 1) * P, decay, [b_ready, tsum_in], X, PB, PT)
            gemm_fm("ob", X, 1024, lambda o, b, m: add_to_h(o, b, m))
            tick(force=True)

    if STAGE >= 4:
        mean_square()
        normed(X, VEC["g_mlp1"], None, [v1_ready, h_ready])
        mlp("m1")
        tick(force=True)
        mean_square()
        for c in range(KC):
            d = DVE(lambda e, c=c: e.scalar_tensor_tensor(HT[:, c, :], HT[:, c, :], VEC["g_final"][:, c:c + 1], rstd.ap[:], ALU.mult, ALU.mult),
                    rstd.ready, v1_ready, h_ready[c])
            h_ready[c] = [d]
            tick()
            square(c)
        rstd.free = [d]

    gm_ready = []

    def mod_gains(layer):
        for k, norm in ((0, "n1"), (1, "n2")):
            sc = MOD[layer][:, 8 + 24 * k:16 + 24 * k]
            d = DVE(lambda e, sc=sc, k=k, norm=norm: e.scalar_tensor_tensor(GM[:, 2 * layer + k, :], sc, 1.0, VEC[f"{norm}_{layer}"], ALU.add, ALU.mult),
                    mod_ready[layer], v1_ready)
        gm_ready[:] = [d]

    def mod(layer, k):
        return MOD[layer][:, 8 * k:8 * k + 8]

    if STAGE >= 5:
        mod_gains(0)
        mod_gains(1)
        mean_square()
        normed(X, GM[:, 0, :], mod(0, 0), [gm_ready, h_ready])
        with ExitStack() as region:
            free = phase_end()
            rope[0] = Buf(sb("rope_b", [P, 2, S], F32, region))
            rope[0].ready = [SP.load(s_rope, lambda e: e.dma_start(rope[0].ap[:], consts["rope_b"]), free)]
            Q = sb("QC", [P, KC, S], F32, region)
            K2 = [sb(f"KC{i}", [P, S], F32, region) for i in range(4)]
            V = sb("VC", [P, NT, 256], F32, region)
            PB = [Buf(sb(f"PC{i}", [P, S], F32, region), free) for i in range(5)]
            PT = [Buf(sb(f"PTC{i}", [P, NT, S], F32, region), free) for i in range(2)]
            a_ready = [free]

            def head_norm(gain, done):
                def evac(o, b, m):
                    q, a = copy_out(b, m)

                    def norm():
                        r = scratch()
                        s = ACT(lambda e: e.activation(r.ap[:], q.ap[:], ACT_F.Square), a, r.free)
                        bm = banks[6]
                        mm = PE(lambda e: e.matmul(bm.ap[:], head_mean[:], r.ap[:], start=True, stop=True), s, bm.free)
                        s = ACT(lambda e: e.activation(r.ap[:], bm.ap[:], ACT_F.Sqrt, bias=eps[:, 0:1]), mm)
                        bm.free = [s]
                        d = DVE(lambda e: e.reciprocal(r.ap[:], r.ap[:]), s)
                        d = DVE(lambda e: e.scalar_tensor_tensor(q.ap[:], q.ap[:], gain, r.ap[:], ALU.mult, ALU.mult), d)
                        r.free = [d]
                        defer(1, lambda: rotate(q, d, 1, P, done(o)))
                    defer(1, norm)
                return evac
            gemm_fm("kc", X, 256, head_norm(VEC["kg"], lambda o: add_twice([K2[2 * o], K2[2 * o + 1]], a_ready)))

            def evac_vc(i, at, k, b, m):
                a = ACT(lambda e: e.activation(V[:, i, at:at + k], b.ap[:, 0:k], ACT_F.Copy), m, free)
                b.free = [a]
                a_ready.append(a)
            gemm_tm("vc", X, 256, evac_vc)
            gemm_fm("qc", X, 1024, head_norm(VEC["qg"], lambda o: add_into(Q[:, o, :], a_ready)))
            tick(force=True)
            attention(
                lambda h, i: Q[64 * (h % 2):64 * (h % 2) + 64, h // 2, i * P:(i + 1) * P],
                lambda h, w: K2[h // 4][64 * (h % 2):64 * (h % 2) + 64, 0:w],
                lambda h, j: V[:, j, 64 * (h // 4):64 * (h // 4) + 64],
                None, lambda i: S, None, a_ready, X, PB, PT)
            gemm_fm("oc", X, 1024, lambda o, b, m: add_to_h(o, b, m, mod(0, 2)))
            tick(force=True)
    if STAGE >= 6:
        mean_square()
        normed(X, GM[:, 1, :], mod(0, 3), [gm_ready, h_ready])
        mlp("m2", mod(0, 5))
        tick(force=True)
    if STAGE >= 7:
        mean_square()
        normed(X, GM[:, 2, :], mod(1, 0), [gm_ready, h_ready])
        with ExitStack() as region:
            free = phase_end()
            VT = sb("VT", [P, NT, 3072], F32, region)
            wsT = sb("wsT", [P, 16, P], F32, region)
            bs = sb("bs", [16, P], F32, region)
            s_g = sem("gmlp_in")
            with ExitStack() as sub:
                row_a = Buf(sb("row_a", [P, 3072], F32, sub))
                row_b = Buf(sb("row_b", [P, 3072], F32, sub))
                s_a, s_b = sem("row_a_in"), sem("row_b_in")
                row_a.ready = [SP.load(s_a, lambda e: e.dma_start(row_a.ap[:], t["gmlp_b_in_2"][0, 3072:6144].partition_broadcast(P)), free)]
                row_b.ready = [SP.load(s_b, lambda e: e.dma_start(row_b.ap[:], t["gmlp_ln_g_2"][0].partition_broadcast(P)), free)]
                bs_in = SP.load(s_g, lambda e: e.dma_start(bs[:], t["gmlp_b_s_2"][0]), free)
                s_w = [sem(f"ws_in{i}") for i in range(2)]
                turned = []

                def turn_ws(k):
                    w = tmp[k % 2]
                    ld = SP.load(s_w[k % 2], lambda e: e.dma_start(
                        w.ap[:].rearrange("p (g q) -> p g q", q=P),
                        t["gmlp_w_s_2"][0, 4 * k:4 * k + 4].rearrange("g p q -> p g q")), w.free)

                    def turn_now():
                        b = banks[4 + k % 2]
                        for g in range(4):
                            m = PE(lambda e: e.transpose(b.ap[:, g * P:(g + 1) * P], w.ap[:, g * P:(g + 1) * P], ident[:]), ld, b.free)
                        w.free = [m]
                        d = DVE(lambda e: e.tensor_copy(wsT[:, 4 * k:4 * k + 4, :].rearrange("p g q -> p (g q)"), b.ap[:]), m, free)
                        b.free = [d]
                        turned.append(d)
                    defer(6, turn_now)
                for k in range(4):
                    defer(4 + 8 * k, lambda k=k: turn_ws(k))
                v_ready = [[] for _ in range(NT)]

                def evac_gv(i, at, k, b, m):
                    d = DVE(lambda e: e.tensor_tensor(VT[:, i, at:at + k], b.ap[:, 0:k], row_a.ap[:, at:at + k], ALU.add), m, row_a.ready)
                    b.free = [d]
                    a = ACT(lambda e: e.activation(VT[:, i, at:at + k], VT[:, i, at:at + k], ACT_F.Gelu), d)
                    v_ready[i].append(a)
                    if at % 512:
                        s = DVE(lambda e, f=at // 512: e.bn_stats(bst[:, i, f, :], VT[:, i, 512 * f:512 * f + 512]), v_ready[i])
                        v_ready[i] = [s]
                gemm_tm("gv", X, 3072, evac_gv)
                row_a.ready = [SP.load(s_a, lambda e: e.dma_start(row_a.ap[:], t["gmlp_ln_b_2"][0].partition_broadcast(P)), DVE.last())]
                for i in range(NT):
                    d = DVE(lambda e, i=i: e.bn_aggr(mv[:, i, :], bst[:, i, :, :]), v_ready[i])
                a = ACT(lambda e: e.activation(rsv[:], mv[:, :, 1], ACT_F.Sqrt, bias=eps[:, 0:1]), d)
                d = DVE(lambda e: e.reciprocal(rsv[:], rsv[:]), a)
                d = DVE(lambda e: e.scalar_tensor_tensor(nmr[:], mv[:, :, 0], -1.0, rsv[:], ALU.mult, ALU.mult), d)
                vn = []
                for f in range(6):
                    for i in range(NT):
                        z = VT[:, i, 512 * f:512 * f + 512]
                        a = ACT(lambda e: e.activation(z, z, ACT_F.Identity, bias=nmr[:, i:i + 1], scale=rsv[:, i:i + 1]), d)
                        d2 = DVE(lambda e, z=z, f=f: e.tensor_tensor(z, z, row_b.ap[:, 512 * f:512 * f + 512], ALU.mult), a, row_b.ready)
                        g = (DVE if i == 3 else POOL)(lambda e, z=z, f=f: e.tensor_tensor(z, z, row_a.ap[:, 512 * f:512 * f + 512], ALU.add), d2, row_a.ready)
                        vn.append(g)
            free = phase_end()
            Y = Split(sb("Yhi", [P, KC, S], F32R, region), sb("Ylo", [P, KC, S], F32R, region), free)

            def mix(j, q, a, write_after):
                b = banks[4 + j % 2]
                parts = [(0, P, (P * j) // 192)] if (P * j) // 192 == (P * j + P - 1) // 192 else [
                    (0, 64, (P * j) // 192), (64, 64, (P * j + 64) // 192)]
                n = 0
                for o, rows, g in parts:
                    PE(lambda e, o=o, rows=rows, g=g: e.matmul(
                        b.ap[o:o + rows, :].rearrange("r (i q) -> r i q", q=P),
                        ident[0:16, g:g + 1].to_broadcast([16, rows]), bs[:].unsqueeze(1).to_broadcast([16, NT, P]),
                        start=True, stop=False, skip_group_check=True), b.free, bs_in, vn[NT * (j // 4):NT * (j // 4) + NT], turned)
                    for i in range(NT):
                        m = PE(lambda e, o=o, rows=rows, g=g, i=i: e.matmul(
                            b.ap[o:o + rows, i * P:(i + 1) * P], VT[:, i, P * j + o:P * j + o + rows], wsT[:, g, :],
                            start=False, stop=(i == NT - 1), skip_group_check=True))
                d = DVE(lambda e: e.tensor_tensor(q.ap[:], b.ap[:], q.ap[:], ALU.mult), m, a)
                b.free = [d]
                c = j % 8
                a2 = ACT(lambda e: e.activation(Y.hi[:, c, :], q.ap[:], ACT_F.Copy), d, write_after)
                d = DVE(lambda e: e.tensor_tensor(Y.lo[:, c, :], q.ap[:], Y.hi[:, c, :].bitcast(F32), ALU.subtract), a2)
                q.free = [d]
                Y.ready[c] = [a2, d]
            for g in range(3):
                write_after = list(Y.free)

                def evac_gu(o, b, m, g=g, write_after=write_after):
                    q = hold()
                    j = 8 * g + o
                    a = ACT(lambda e: e.activation(q.ap[:], b.ap[:], ACT_F.Gelu, bias=VEC["b_in"][:, j:j + 1]), m, q.free)
                    b.free = [a]
                    defer(2, lambda: mix(j, q, a, write_after))
                gemm_fm("gu", X, 1024, evac_gu)
                tick(force=True)
                gemm_fm("go", Y, 1024, lambda o, b, m: add_to_h(o, b, m, mod(1, 2), last=(g == 2)))
                tick(force=True)
    if STAGE >= 8:
        mean_square()
        normed(X, GM[:, 3, :], mod(1, 3), [gm_ready, h_ready])
        mlp("m3", mod(1, 5))
        tick(force=True)

    s_out = sem("out_done")
    with ExitStack() as region:
        free = phase_end()
        O = sb("O", [P, NT, D], F32, region)
        for i in range(NT):
            vs = []
            for half in range(2):
                b = gemm_bank()
                for c in range(4):
                    cc = 4 * half + c
                    m = PE(lambda e, c=c, cc=cc, i=i, b=b: e.transpose(b.ap[:, c * P:(c + 1) * P], HT[:, cc, i * P:(i + 1) * P], ident[:]), h_ready[cc], b.free)
                dst = O[:, i, 512 * half:512 * half + 512]
                if half:
                    v = DVE(lambda e, dst=dst, b=b: e.tensor_copy(dst, b.ap[:]), m, free)
                else:
                    v = ACT(lambda e, dst=dst, b=b: e.activation(dst, b.ap[:], ACT_F.Copy), m, free)
                b.free = [v]
                vs.append(v)
            o_done = SP.load(s_out, lambda e, i=i: e.dma_start(out[0, i * P:(i + 1) * P, :], O[:, i, :]), vs)
    SP.wait([o_done])


def shape_constants():
    f = np.float32
    i = np.arange(P)
    inv = (1.0 / (f(10000.0) ** (np.arange(0, 64, 2, dtype=f) / f(64)))).astype(f)
    ang = np.arange(S, dtype=f)[:, None] * inv[None, :]
    c, s = np.cos(ang).T.astype(f), np.sin(ang).T.astype(f)
    rope_a = np.stack([np.tile(c, (4, 1)), np.concatenate([-s, s, -s, s])], 1)
    perm_half = np.zeros((P, P), f)
    perm_half[i, i ^ 32] = 1
    perm_pair = np.zeros((P, P), f)
    perm_pair[i, i ^ 1] = 1
    tok = np.arange(S)
    row = (tok // 64 - (S // 64) // 2).astype(f)
    col = (tok % 64 - 32).astype(f)
    freq = (f(10000.0) ** (-np.arange(16, dtype=f) / f(16))).astype(f)
    ang = np.concatenate([row[:, None] * freq, col[:, None] * freq], -1)
    c, s = np.cos(ang).T.astype(f), np.sin(ang).T.astype(f)
    sign = np.where(i % 2, 1.0, -1.0).astype(f)[:, None]
    rope_b = np.stack([c[(i % 64) // 2], sign * s[(i % 64) // 2]], 1)
    tri = np.zeros((P, S), f)
    tri[:, 384:] = np.where(i[None, :] > i[:, None], -BIG, 0.0)
    tsum = np.ones((P, S), f)
    tsum[:, 0:P] = i[:, None] <= i[None, :]
    one_hot = np.tile(np.eye(32, 16, dtype=f), (4, 1))
    return {
        "ident": np.eye(P, dtype=f), "head_mean": np.kron(np.eye(2), np.full((64, 64), 1 / 64)).astype(f),
        "perm_half": perm_half, "perm_pair": perm_pair, "one_hot": one_hot,
        "rope_a": rope_a.astype(f), "rope_b": rope_b.astype(f), "tri": tri, "tsum": tsum,
    }


def kernel(**inputs):
    import numpy as _np
    import concourse.bacc as _bacc
    from concourse import mybir as _mybir
    from concourse.bass_utils import run_bass_kernel_spmd as _run

    nc = _bacc.Bacc("TRN2", target_bir_lowering=False, num_devices=1)
    arrays, t, consts = {}, {}, {}
    for name in inputs:
        a = _np.ascontiguousarray(inputs[name])
        arrays[f"in_{name}"] = a
        t[name] = nc.dram_tensor(f"in_{name}", a.shape, _mybir.dt.from_np(a.dtype), kind="ExternalInput").ap()
    for name, a in shape_constants().items():
        a = _np.ascontiguousarray(a)
        arrays[f"const_{name}"] = a
        consts[name] = nc.dram_tensor(f"const_{name}", a.shape, _mybir.dt.from_np(a.dtype), kind="ExternalInput").ap()
    out = nc.dram_tensor("out_0", (1, S, D), F32, kind="ExternalOutput").ap()
    program(nc, t, consts, out)
    r = _run(nc, [arrays], core_ids=[0])
    return r.results[0]["out_0"]
```

```python
from contextlib import ExitStack

import numpy as np

import concourse.bass as bass
from concourse import mybir

ALU = mybir.AluOpType
ACT_F = mybir.ActivationFunctionType
F32 = mybir.dt.float32
F32R = mybir.dt.float32r

P = 128
S = 512
D = 1024
NT = S // P
KC = D // P
UC = 256
EPS = 1e-6
BIG = 1e30
USED = -3e38
SHUT = -1e38
STAGE = 99


class Engine:

    def __init__(self, sem):
        self.sem, self.count, self.seen, self.eng = sem, 0, {}, None

    def wait(self, waits):
        for sem, value in flat(waits):
            if self.seen.get(sem.name, 0) < value:
                self.seen[sem.name] = value
                self.eng.wait_ge(sem, value)

    def __call__(self, issue, *waits, inc=True):
        self.wait(waits)
        done = issue(self.eng)
        if not inc:
            return None
        done.then_inc(self.sem, 1)
        self.count += 1
        return (self.sem, self.count)

    def last(self):
        return (self.sem, self.count)


class Loader(Engine):

    def __init__(self):
        self.at, self.seen, self.eng = {}, {}, None

    def load(self, sem, issue, *waits):
        self.wait(waits)
        issue(self.eng).then_inc(sem, 16)
        self.at[sem.name] = self.at.get(sem.name, 0) + 16
        return (sem, self.at[sem.name])


def flat(waits):
    for w in waits:
        if w is None:
            continue
        if isinstance(w, tuple) and len(w) == 2 and isinstance(w[1], int):
            yield w
        else:
            yield from flat(w)


class Buf:

    def __init__(self, ap, free=()):
        self.ap, self.ready, self.free = ap, [], list(free)


class Split:

    def __init__(self, hi, lo, free=()):
        self.hi, self.lo = hi, lo
        self.ready = [[] for _ in range(KC)]
        self.free = list(free)


def program(nc, t, consts, out):
    with ExitStack() as ctx:
        PE, ACT, DVE, POOL = (Engine(ctx.enter_context(nc.semaphore(n))) for n in ("pe", "act", "dve", "pool"))
        SP, ACTQ = Loader(), Loader()
        for engine, issuer in ((PE, nc.tensor), (ACT, nc.scalar), (DVE, nc.vector), (POOL, nc.gpsimd), (SP, nc.sync), (ACTQ, nc.scalar)):
            engine.eng = issuer
        body(nc, ctx, t, consts, out, PE, ACT, DVE, POOL, SP, ACTQ)


def body(nc, ctx, t, consts, out, PE, ACT, DVE, POOL, SP, ACTQ):
    def sem(name):
        return ctx.enter_context(nc.semaphore(name))

    def sb(name, shape, dt=F32, stack=ctx):
        return stack.enter_context(nc.sbuf_tensor(name, shape, dt))

    banks = [Buf(ctx.enter_context(nc.psum_tensor(f"bank{i}", [P, 512], F32))) for i in range(8)]

    HT = sb("HT", [P, KC, S])
    h_ready = [[] for _ in range(KC)]
    X = Split(sb("Xhi", [P, KC, S], F32R), sb("Xlo", [P, KC, S], F32R))
    NRAW, NSP = 2, 2
    raw = [Buf(sb(f"raw{i}", [P, KC, UC])) for i in range(NRAW)]
    raw_sem = [sem(f"raw_in{i}") for i in range(NRAW)]
    whi = [sb(f"whi{i}", [P, KC, UC], F32R) for i in range(NSP)]
    wlo = [sb(f"wlo{i}", [P, KC, UC], F32R) for i in range(NSP)]
    wfree = [[] for _ in range(NSP)]
    tmp = [Buf(sb(f"tmp{i}", [P, S])) for i in range(4)]
    held = [Buf(sb(f"held{i}", [P, S])) for i in range(3)]
    rstd = Buf(sb("rstd", [P, S]))
    rope = [None]
    ident = sb("ident", [P, P])
    ones = sb("ones", [P, P])
    mean = sb("mean", [P, 1])
    rcol = sb("rcol", [P, 2 * NT])
    r2 = sb("r2", [P, 2 * NT])
    FG = sb("FG", [P, KC])
    head_mean = sb("head_mean", [P, P])
    perm = [sb(f"perm{i}", [P, P]) for i in range(2)]
    one_hot = sb("one_hot", [P, 16])
    eps = sb("eps", [P, 1])
    V1 = sb("V1", [P, 114])
    V2 = sb("V2", [P, 96])
    bf = sb("bf", [P, 16])
    cond = sb("cond", [P, 3, KC])
    MOD = [sb(f"MOD{i}", [P, 48]) for i in range(2)]
    GM = sb("GM", [P, 4, KC])
    acc = [Buf(sb(f"acc{i}", [P, UC])) for i in range(2)]
    stats = sb("stats", [P, 6, 4])
    stat = [Buf(stats[:, i, :]) for i in range(6)]
    bst = sb("bst", [P, NT, 6, 6])
    mv = sb("mv", [P, NT, 2])
    rsv = sb("rsv", [P, NT])
    nmr = sb("nmr", [P, NT])

    tmp_at = [0]

    def scratch():
        b = tmp[tmp_at[0] % len(tmp)]
        tmp_at[0] += 1
        return b

    held_at = [0]

    def hold():
        b = held[held_at[0] % len(held)]
        held_at[0] += 1
        return b

    later = []

    def defer(n, fn):
        later.append([n, fn])

    def tick(force=False):
        for item in later:
            item[0] -= 1
        while True:
            due = [item for item in later if force or item[0] <= 0]
            if not due:
                return
            later.remove(due[0])
            due[0][1]()

    s_const = sem("const_in")

    def const(dst, name):
        src = consts[name]
        return SP.load(s_const, lambda e, dst=dst, src=src: e.dma_start(dst, src))

    s_ident = sem("ident_in")
    i_in = SP.load(s_ident, lambda e: e.dma_start(ident[:], consts["ident"]))
    DVE(lambda e: e.memset(mean[:], 1.0 / D))
    DVE(lambda e: e.memset(ones[:], 1.0))
    d_const = DVE(lambda e: e.memset(eps[:], EPS))
    s_vec = sem("vec_in")

    def phase_end():
        return [PE.last(), ACT.last(), DVE.last(), POOL.last()]

    def block_of(w, r0, c0, n):
        return w[r0:r0 + D, c0:c0 + n].rearrange("(c p) n -> p c n", p=P)

    plan = []

    def plan_cols(name, w, c0, n, r0=0):
        for c in range(c0, c0 + n, UC):
            k = min(UC, c0 + n - c)
            plan.append((name, block_of(w, r0, c, k), k))

    ada = [("ada", block_of(t["ada_w_2"][i], 0, c, UC), (i, c // P)) for i in range(2) for c in range(0, 6 * D, UC)]

    def plan_mlp(name, up, down, with_ada):
        start = len(plan)

        def up_g(g):
            plan_cols(name + "u", up, g * D, D)

        def down_g(g):
            plan_cols(name + "d", down, 0, D, r0=g * D)
        for f, g in ((up_g, 0), (up_g, 1), (down_g, 0), (up_g, 2), (down_g, 1), (up_g, 3), (down_g, 2), (down_g, 3)):
            f(g)
        if with_ada:
            units = plan[start:]
            del plan[start:]
            for i, u in enumerate(units):
                plan.append(u)
                if 1 <= i < 25:
                    plan.append(ada.pop(0))

    wa = t["w_in_a"][0]
    plan_cols("qi", wa, 1536, 512)
    plan_cols("ki", wa, 2048, 72)
    plan_cols("qa", wa, 0, 1024)
    plan_cols("ka", wa, 1024, 256)
    plan_cols("va", wa, 1280, 256)
    plan_cols("oa", t["w_o_a"][0], 0, 1024)
    plan_mlp("m0", t["w_up"][0], t["w_down"][0], True)
    wk = t["w_kv_b"]
    plan_cols("kb", wk, 0, 1024)
    plan_cols("fb", wk, 2048, 16)
    plan_cols("vb", wk, 1024, 1024)
    plan_cols("qb", t["w_q_b"][0], 0, 1024)
    plan_cols("ob", t["w_o_b"][0], 0, 1024)
    plan_mlp("m1", t["w_up"][1], t["w_down"][1], True)
    wq = t["attn_w_qkv_2"][0]
    plan_cols("kc", wq, 1024, 256)
    plan_cols("vc", wq, 1280, 256)
    plan_cols("qc", wq, 0, 1024)
    plan_cols("oc", t["attn_w_o_2"][0], 0, 1024)
    plan_mlp("m2", t["mlp_w_in_2"][0], t["mlp_w_out_2"][0], False)
    wg = t["gmlp_w_in_2"][0]
    plan_cols("gv", wg, 3072, 3072)
    for g in range(3):
        plan_cols("gu", wg, g * D, D)
        plan_cols("go", t["gmlp_w_out_2"][0], 0, D, r0=g * D)
    plan_mlp("m3", t["mlp_w_in_2"][1], t["mlp_w_out_2"][1], False)

    loaded, split_at, used = [0], [0], [0]
    loads, splits = {}, {}
    mod_ready = [[], []]
    v2_ready = []
    cond_ready = []

    def load_next():
        n = loaded[0]
        if n >= len(plan):
            return
        name, src, k = plan[n]
        k = UC if name == "ada" else k
        place = raw[n % NRAW]
        loads[n] = SP.load(raw_sem[n % NRAW], lambda e, place=place, src=src, k=k: e.dma_start(place.ap[:, :, 0:k], src), place.free)
        place.free = []
        loaded[0] += 1

    gemm_no = [0]

    def split_next():
        while split_at[0] < len(plan):
            n = split_at[0]
            split_at[0] += 1
            if n >= loaded[0]:
                load_next()
            name, _, k = plan[n]
            place = raw[n % NRAW]
            if name == "ada":
                ada_unit(place, loads[n], *k)
                load_next()
                continue
            slot = gemm_no[0] % NSP
            gemm_no[0] += 1
            hi, lo = whi[slot], wlo[slot]
            ready = []
            for c0, c1 in ((0, KC // 2), (KC // 2, KC)):
                a = ACT(lambda e: e.activation(hi[:, c0:c1, 0:k], place.ap[:, c0:c1, 0:k], ACT_F.Copy), loads[n], wfree[slot])
                p = POOL(lambda e: e.tensor_tensor(
                    lo[:, c0:c1, 0:k], place.ap[:, c0:c1, 0:k], hi[:, c0:c1, 0:k].bitcast(F32), ALU.subtract), a, wfree[slot])
                ready += [[a, p]] * (KC // 2)
            place.free = [p]
            splits[n] = (name, slot, ready)
            load_next()
            return

    def ada_unit(place, arrived, layer, col):
        a = acc[(col // 2) % 2]
        cd = cond[:, 2, :]
        tok = DVE(lambda e: e.tensor_scalar(a.ap[:], place.ap[:, 0, :], cd[:, 0:1], None, ALU.mult), arrived, cond_ready, a.free)
        for c in range(1, KC):
            tok = DVE(lambda e, c=c: e.scalar_tensor_tensor(a.ap[:], place.ap[:, c, :], cd[:, c:c + 1], a.ap[:], ALU.mult, ALU.add), tok)
        place.free = [tok]
        a.ready = [tok]

        def sums():
            b = banks[7]
            for j in range(2):
                m = PE(lambda e, j=j: e.matmul(b.ap[:, j:j + 1], a.ap[:, j * P:(j + 1) * P], ones[:, 0:1], start=True, stop=True),
                       a.ready, b.free)
            a.free = [m]
            d = DVE(lambda e: e.tensor_tensor(MOD[layer][:, col:col + 2], b.ap[:, 0:2],
                                              V2[:, layer * 48 + col:layer * 48 + col + 2], ALU.add), m, v2_ready)
            b.free = [d]
            mod_ready[layer] = [d]
        defer(3, sums)

    current = []

    def unit(name):
        while used[0] not in splits:
            if plan[used[0]][0] == "ada" and used[0] < split_at[0]:
                used[0] += 1
                continue
            split_next()
        n = used[0]
        used[0] += 1
        got, slot, ready = splits.pop(n)
        assert got == name, (got, name)
        return slot, ready

    gb = [0]

    def gemm_bank():
        b = banks[gb[0] % 4]
        gb[0] += 1
        return b

    def gemm_fm(name, x, n_cols, evac, first=False):
        at = 0
        if first:
            gemm_fm_first(name, x, evac)
            at = UC
        while at < n_cols:
            slot, ready = unit(name)
            split_next()
            k = min(UC, n_cols - at)
            for j in range(0, k, P):
                m_cols = min(P, k - j)
                b = gemm_bank()
                n = 0
                for c in range(KC):
                    for w, v in ((whi, x.hi), (whi, x.lo), (wlo, x.hi)):
                        m = PE(lambda e, w=w, v=v, c=c, j=j, n=n, b=b, m_cols=m_cols: e.matmul(
                            b.ap[0:m_cols, :], w[slot][:, c, j:j + m_cols], v[:, c, :], start=(n == 0), stop=(n == 3 * KC - 1)),
                            ready[c], b.free, x.ready[c], inc=(n == 3 * KC - 1))
                        n += 1
                x.free = [m]
                wfree[slot] = [m]
                tick()
                evac((at + j) // P, b, m)
            at += k

    def gemm_fm_first(name, x, evac):
        slot, ready = unit(name)
        split_next()
        pair = [gemm_bank(), gemm_bank()]
        for c in range(KC):
            for j, b in enumerate(pair):
                for n, (w, v) in enumerate(((whi, x.hi), (whi, x.lo), (wlo, x.hi))):
                    m = PE(lambda e: e.matmul(b.ap[:], w[slot][:, c, j * P:(j + 1) * P], v[:, c, :],
                                              start=(c == 0 and n == 0), stop=(c == KC - 1 and n == 2)),
                           ready[c], b.free, x.ready[c], inc=(c == KC - 1 and n == 2))
                    if m:
                        b.ready = [m]
        x.free = [m]
        wfree[slot] = [m]
        for j, b in enumerate(pair):
            tick()
            evac(j, b, b.ready)

    def gemm_tm(name, x, n_cols, evac):
        at = 0
        while at < n_cols:
            slot, ready = unit(name)
            split_next()
            k = min(UC, n_cols - at)
            for i in range(NT):
                b = gemm_bank()
                n = 0
                for c in range(KC):
                    for v, w in ((x.hi, whi), (x.hi, wlo), (x.lo, whi)):
                        m = PE(lambda e, w=w, v=v, c=c, i=i, n=n, b=b, k=k: e.matmul(
                            b.ap[:, 0:k], v[:, c, i * P:(i + 1) * P], w[slot][:, c, 0:k], start=(n == 0), stop=(n == 3 * KC - 1)),
                            ready[c], b.free, x.ready[c], inc=(n == 3 * KC - 1))
                        n += 1
                x.free = [m]
                wfree[slot] = [m]
                tick()
                evac(i, at, k, b, m)
            at += k

    def square(c, gain=None):
        b, q = banks[6], hold()
        a = ACT(lambda e: e.activation(q.ap[:], HT[:, c, :], ACT_F.Square), h_ready[c], q.free)

        def add():
            for i in range(NT):
                m = PE(lambda e: e.matmul(b.ap[:, i:i + 1], q.ap[:, i * P:(i + 1) * P], mean[:], start=(c == 0 and i == 0),
                                          stop=(c == KC - 1 and i == NT - 1), skip_group_check=True), a, b.free, d_const)
            q.free = [m]
        defer(1, add)
        if gain is None:
            return
        q2 = hold()
        a2 = ACT(lambda e: e.activation(q2.ap[:], HT[:, c, :], ACT_F.Square, scale=gain[:, c:c + 1]), h_ready[c], q2.free)

        def add_gained():
            for i in range(NT):
                m = PE(lambda e: e.matmul(b.ap[:, NT + i:NT + i + 1], q2.ap[:, i * P:(i + 1) * P], mean[:], start=False,
                                          stop=(c == KC - 1 and i == NT - 1), skip_group_check=True), a2)
            q2.free = [m]
        defer(1, add_gained)

    def mean_square():
        tick(force=True)
        m = PE.last()
        a = ACT(lambda e: e.activation(rcol[:, 0:NT], banks[6].ap[:, 0:NT], ACT_F.Sqrt, bias=eps[:, 0:1]), m)
        banks[6].free = [a]
        spread(DVE(lambda e: e.reciprocal(rcol[:, NT:2 * NT], rcol[:, 0:NT]), a), rcol[:, NT:2 * NT])

    def to_rows(b, ready, col):
        for i in range(NT):
            m = PE(lambda e: e.matmul(b.ap[:, i * P:(i + 1) * P], col[:, i:i + 1].to_broadcast([P, P]), ident[:],
                                      start=True, stop=True), ready, i_in, b.free)
        return m

    def spread(ready, col):
        b = banks[6]
        m = to_rows(b, ready, col)
        a = ACT(lambda e: e.activation(rstd.ap[:], b.ap[:], ACT_F.Copy), m, rstd.free)
        b.free = [a]
        rstd.ready = [a]

    def normed(x, gain, shift, ready):
        def first(c):
            q = scratch()
            d = DVE(lambda e: e.scalar_tensor_tensor(q.ap[:], HT[:, c, :], gain[:, c:c + 1], rstd.ap[:], ALU.mult, ALU.mult),
                    rstd.ready, ready, q.free)
            rstd.free = [d]
            if shift is None:
                a = ACT(lambda e: e.activation(x.hi[:, c, :], q.ap[:], ACT_F.Copy), d, x.free)
            else:
                a = ACT(lambda e: e.activation(x.hi[:, c, :], q.ap[:], ACT_F.Identity, bias=shift[:, c:c + 1]), d, x.free)
            q.free = [a]
            return c, q, d, a

        def second(c, q, d, a):
            hi, lo = x.hi[:, c, :].bitcast(F32), x.lo[:, c, :]
            if shift is not None:
                p = DVE(lambda e: e.scalar_tensor_tensor(lo, q.ap[:], shift[:, c:c + 1], hi, ALU.add, ALU.subtract), a)
            elif c % 3 == 1:
                p = POOL(lambda e: e.tensor_tensor(lo, q.ap[:], hi, ALU.subtract), d, a)
            else:
                p = DVE(lambda e: e.tensor_tensor(lo, q.ap[:], hi, ALU.subtract), a)
            q.free = [p]
            x.ready[c] = [a, p]
        behind = None
        for c in range(KC):
            now = first(c)
            if behind:
                second(*behind)
            behind = now
        second(*behind)

    def add_to_h(o, b, m, gate=None, ready=(), last=True):
        if gate is None:
            d = DVE(lambda e: e.tensor_tensor(HT[:, o, :], b.ap[:], HT[:, o, :], ALU.add), m, h_ready[o])
        else:
            d = DVE(lambda e: e.scalar_tensor_tensor(HT[:, o, :], b.ap[:], gate[:, o:o + 1], HT[:, o, :], ALU.mult, ALU.add), m, h_ready[o], ready)
        b.free = [d]
        h_ready[o] = [d]
        if last:
            square(o, VEC["g_final"] if last == "final" else None)

    def mlp(name, gate=None, ready=(), at_end=lambda: None):
        with ExitStack() as region:
            free = phase_end()
            H = [Split(sb(f"{name}Hhi{i}", [P, KC, S], F32R, region), sb(f"{name}Hlo{i}", [P, KC, S], F32R, region), free) for i in range(2)]

            def up(g):
                h = H[g % 2]
                write_after = list(h.free)

                def evac(o, b, m):
                    q, r = scratch(), scratch()
                    a = ACT(lambda e: e.activation(q.ap[:], b.ap[:], ACT_F.Relu), m, q.free)
                    b.free = [a]
                    a2 = ACT(lambda e: e.activation(h.hi[:, o, :], q.ap[:], ACT_F.Square), a, write_after)
                    d = DVE(lambda e: e.tensor_tensor(r.ap[:], q.ap[:], q.ap[:], ALU.mult), a, r.free)
                    q.free = [a2, d]
                    d = DVE(lambda e: e.tensor_tensor(h.lo[:, o, :], r.ap[:], h.hi[:, o, :].bitcast(F32), ALU.subtract), a2, d, write_after)
                    r.free = [d]
                    h.ready[o] = [a2, d]
                gemm_fm(name + "u", X, D, evac, first=(g == 0))

            def down(g):
                gemm_fm(name + "d", H[g % 2], D, lambda o, b, m: add_to_h(o, b, m, gate, ready, g == 3 and {"m1": "final", "m3": False}.get(name, True)))
            for f, g in ((up, 0), (up, 1), (down, 0), (up, 2), (down, 1), (up, 3), (down, 2), (down, 3)):
                if (f, g) == (down, 3):
                    at_end()
                f(g)

    rb = [0]

    def rotate(src, ready, p, rows, done):
        b, CS = banks[4], rope[0]
        rb[0] += 1
        m = PE(lambda e: e.matmul(b.ap[0:rows, :], perm[p][0:rows, 0:rows], src.ap[0:rows, :], start=True, stop=True), ready, b.free, c_ready)
        r = scratch()
        d = DVE(lambda e: e.tensor_tensor(r.ap[0:rows, :], b.ap[0:rows, :], CS.ap[0:rows, 1, :], ALU.mult), m, r.free, CS.ready)
        b.free = [d]
        q = POOL(lambda e: e.tensor_tensor(src.ap[0:rows, :], src.ap[0:rows, :], CS.ap[0:rows, 0, :], ALU.mult), m, ready, CS.ready)
        d = done(src, r, [d, q])
        src.free, r.free = [d], [d]

    def add_into(dst, ready_list, on=None):
        def done(x1, x2, ready):
            d = (on or DVE)(lambda e: e.tensor_tensor(dst, x1.ap[:], x2.ap[:], ALU.add), ready)
            ready_list.append(d)
            return d
        return done

    def add_twice(dsts, ready_list):
        def done(x1, x2, ready):
            for i, dst in enumerate(dsts):
                for half in range(2):
                    d = DVE(lambda e, i=i, half=half, dst=dst: e.tensor_tensor(
                        dst[64 * half:64 * half + 64, :], x1.ap[64 * i:64 * i + 64, :], x2.ap[64 * i:64 * i + 64, :], ALU.add), ready)
            ready_list.append(d)
            return d
        return done

    def copy_out(b, m, rows=P):
        q = hold()
        a = ACT(lambda e: e.activation(q.ap[0:rows, :], b.ap[0:rows, :], ACT_F.Copy), m, q.free)
        b.free = [a]
        return q, a

    LAG = 4
    mask_ready = {}

    def attention(heads_q, heads_k, heads_v, mask, width, extra, ready, x, PB, PT, steps=None, between=None):
        scale = 0.125
        steps = steps or [(h, i) for h in range(16) for i in range(NT)]
        first_of = [steps.index((h, 0)) for h in range(16)] + [len(steps) + 8] * 2
        last_of = [max(n for n, s in enumerate(steps) if s[0] == h) for h in range(16)]
        values_at = {}
        for h in range(16):
            for j in range(NT):
                values_at.setdefault(LAG + min(last_of[h] + min(2 + j, 4), first_of[h + 2] - 1), []).append((h, j))
        prob = {}
        write_after = list(x.free)

        def scores(n):
            h, i = steps[n]
            w = width(i)
            b, pb, st = banks[n % 3], PB[n % len(PB)], stat[n % len(stat)]
            q, k = heads_q(h, i), heads_k(h, w)
            e2 = extra(h, i, w) if extra else None
            m = PE(lambda e: e.matmul(b.ap[:, 0:w], q, k, start=True, stop=e2 is None), ready, b.free)
            seen = mask_ready.get(i) if mask else None
            if e2:
                l2, r2, tok = e2
                m = PE(lambda e: e.matmul(b.ap[:, 0:w], l2, r2, start=False, stop=True), tok)
                extra_free(h, m)
            mk = mask(i, w) if mask else None
            if mk is not None:
                d = DVE(lambda e: e.tensor_tensor_reduce(pb.ap[:, 0:w], b.ap[:, 0:w], mk, -scale, 3e38, ALU.add, ALU.min, st.ap[:, 0:1]),
                        m, seen, pb.free, st.free)
            else:
                d = DVE(lambda e: e.tensor_scalar(pb.ap[:, 0:w], b.ap[:, 0:w], -scale, None, ALU.mult, ALU.min, accum_out=st.ap[:, 0:1]),
                        m, pb.free, st.free)
            b.free = [d]
            a = ACT(lambda e: e.activation(pb.ap[:, 0:w], pb.ap[:, 0:w], ACT_F.Exp, bias=st.ap[:, 0:1], scale=-1.0, accum_out=st.ap[:, 1:2]), d)
            prob[n] = a

        def divide(n):
            w = width(steps[n][1])
            pb, st = PB[n % len(PB)], stat[n % len(stat)]
            d = DVE(lambda e: e.reciprocal(st.ap[:, 2:3], st.ap[:, 1:2]), prob[n])
            g = DVE(lambda e: e.tensor_scalar(pb.ap[:, 0:w], pb.ap[:, 0:w], st.ap[:, 2:3], None, ALU.mult), d)
            st.free = [g]
            prob[n] = g

        def turn(n):
            h, i = steps[n]
            w = width(i)
            b, pb, pt = banks[(3, 4, 7)[n % 3]], PB[n % len(PB)], PT[h % 2]
            for j in range(0, w, P):
                m = PE(lambda e, j=j: e.transpose(b.ap[:, j:j + P], pb.ap[:, j:j + P], ident[:]), prob[n], b.free)
            pb.free = [m]
            dst = pt.ap[:, 0:w // P, i * P:(i + 1) * P]
            src = b.ap[:, 0:w].rearrange("p (j q) -> p j q", q=P)
            if n % 4:
                v = ACT(lambda e: e.activation(dst, src, ACT_F.Copy), m, pt.free)
            else:
                v = DVE(lambda e: e.tensor_copy(dst, src), m, pt.free)
            b.free = [v]
            if i == 0:
                pt.ready = []
            pt.ready.append(v)

        def values(h, j):
            b, pt = banks[5 + (h // 2) % 2], PT[h % 2]
            o = 64 * (h % 2)
            full = width(0) == S
            q0 = 0 if full else j * P
            v = heads_v(h, j)
            m = PE(lambda e: e.matmul(b.ap[o:o + 64, q0:S], v, pt.ap[:, j, q0:S], start=(j == 0), stop=(j == NT - 1)), pt.ready, b.free)
            pt.free = [m]
            if h % 2 and j == NT - 1:
                c = h // 2
                a = ACT(lambda e: e.activation(x.hi[:, c, :], b.ap[:], ACT_F.Copy), m, write_after)
                d = DVE(lambda e: e.tensor_tensor(x.lo[:, c, :], b.ap[:], x.hi[:, c, :].bitcast(F32), ALU.subtract), a)
                b.free = [d]
                x.ready[c] = [a, d]

        for n in range(len(steps) + LAG + 4):
            if LAG <= n < len(steps) + LAG:
                turn(n - LAG)
            if n < len(steps):
                if between:
                    between(n)
                scores(n)
            if 1 <= n < len(steps) + 1:
                divide(n - 1)
            for h, j in values_at.get(n, ()):
                values(h, j)

    extra_hook = [None]

    def extra_free(h, m):
        extra_hook[0](h, m)

    with ExitStack() as region:
        XT = sb("XT", [P, NT, D], F32, region)
        junk = sb("junk", [P, D], F32, region)
        R1 = sb("R1", [114, P], F32, region)
        R2 = sb("R2", [96, P], F32, region)
        vec_loads = []
        s_x = [sem(f"x_in{i}") for i in range(NT)]
        xin = [SP.load(s_x[i], lambda e, i=i: e.dma_start(XT[:, i, :], t["x"][0, i * P:(i + 1) * P, :])) for i in range(NT)]
        for i in range(NT):
            a = ACT(lambda e: e.activation(junk[:], XT[:, i, :], ACT_F.Square, accum_out=rcol[:, i:i + 1]), xin[i], ACT.last())
        a = ACT(lambda e: e.activation(rcol[:, 0:NT], rcol[:, 0:NT], ACT_F.Sqrt, bias=eps[:, 0:1], scale=1.0 / D), d_const, a)
        root = DVE(lambda e: e.reciprocal(rcol[:, NT:2 * NT], rcol[:, 0:NT]), a)
        VEC = {}
        row = 0
        for names, src, n in (
            (("g_attn_a",), t["g_attn_a"][0], 8), (("g_kv",), t["g_kv"], 8), (("g_attn_b",), t["g_attn_b"][0], 8),
            (("g_mlp0", "g_mlp1"), t["g_mlp"], 8), (("g_final",), t["g_final"], 8),
            (("n1_0", "n1_1"), t["norm1_g_2"], 8), (("n2_0", "n2_1"), t["norm2_g_2"], 8),
            (("c",), t["c_2"][0], 8), (("b_in",), t["gmlp_b_in_2"][0, 0:3072], 24),
        ):
            for k, name in enumerate(names):
                VEC[name] = V1[:, row + k * n:row + (k + 1) * n]
            n *= len(names)
            flat_src = src.rearrange("(r k) -> r k", k=P) if len(names) == 1 else src.rearrange("l (r k) -> (l r) k", k=P)
            vec_loads.append((R1[row:row + n, :], flat_src))
            row += n
        for name, src in (("qg", t["attn_q_norm_g_2"]), ("kg", t["attn_k_norm_g_2"])):
            for half in range(2):
                vec_loads.append((R1[row:row + 1, 64 * half:64 * half + 64], src))
            VEC[name] = V1[:, row:row + 1]
            row += 1
        vec_loads.append((R2[:], t["ada_b_2"].rearrange("l (r k) -> (l r) k", k=P)))
        vec_loads.append((bf[:], t["b_f"].partition_broadcast(P)))
        for k, (dst, src) in enumerate(vec_loads):
            if k == 7:
                load_next()
                load_next()
            vec_in = SP.load(s_vec, lambda e, dst=dst, src=src: e.dma_start(dst, src))
        const(head_mean[:], "head_mean")
        const(perm[0][:], "perm_half")
        const(perm[1][:], "perm_pair")
        c_ready = const(one_hot[:], "one_hot")
        for c in range(KC):
            b = gemm_bank()
            for i in range(NT):
                m = PE(lambda e, i=i, c=c, b=b: e.transpose(b.ap[:, i * P:(i + 1) * P], XT[:, i, c * P:(c + 1) * P], ident[:]), xin[i], i_in, b.free)
            if c % 2:
                v = DVE(lambda e, c=c, b=b: e.tensor_copy(HT[:, c, :], b.ap[:]), m)
            else:
                v = ACT(lambda e, c=c, b=b: e.activation(HT[:, c, :], b.ap[:], ACT_F.Copy), m)
            b.free = [v]
            h_ready[c] = [v]
            if c == 3:
                spread(root, rcol[:, NT:2 * NT])
        b = banks[4]
        m = PE(lambda e: e.transpose(b.ap[:, 0:114], R1[:], ident[0:114, 0:114]), vec_in, i_in)
        d = DVE(lambda e: e.tensor_copy(V1[:], b.ap[:, 0:114]), m)
        b.free = [d]
        v1_ready = [d]
        b = banks[5]
        m = PE(lambda e: e.transpose(b.ap[:, 0:96], R2[:], ident[0:96, 0:96]), vec_in)
        d = DVE(lambda e: e.tensor_copy(V2[:], b.ap[:, 0:96]), m)
        b.free = [d]
        v2_ready.append(d)
        normed(X, VEC["g_attn_a"], None, [v1_ready, h_ready])
        a = ACT(lambda e: e.activation(cond[:, 0, :], VEC["c"], ACT_F.Exp, scale=-1.0), v1_ready)
        d = DVE(lambda e: e.tensor_scalar(cond[:, 0, :], cond[:, 0, :], 1.0, None, ALU.add), a)
        d = DVE(lambda e: e.reciprocal(cond[:, 1, :], cond[:, 0, :]), d)
        d = DVE(lambda e: e.tensor_tensor(cond[:, 2, :], cond[:, 1, :], VEC["c"], ALU.mult), d)
        cond_ready.append(d)

    s_rope = sem("rope_in")
    with ExitStack() as region:
        free = phase_end()
        Q = sb("QA", [P, KC, S], F32, region)
        K2 = [sb(f"KA{i}", [P, S], F32, region) for i in range(4)]
        V = sb("VA", [P, NT, 256], F32, region)
        PB = [Buf(sb(f"PA{i}", [P, S], F32, region), free) for i in range(5)]
        PT = [Buf(sb(f"PTA{i}", [P, NT, S], F32, region), free) for i in range(2)]
        QI = sb("QI", [P, 4, S], F32, region)
        KI = sb("KI", [P, S], F32, region)
        WI = sb("WI", [P, NT, 8], F32, region)
        SC = [Buf(sb(f"SC{i}", [P, S], F32, region), free) for i in range(3)]
        SC2 = Buf(sb("SCW", [P, S], F32, region), free)
        top = Buf(sb("top", [P, 8], F32, region), free)
        M = [sb(f"MA{i}", [P, (i + 1) * P], F32, region) for i in range(NT)]
        rope[0] = Buf(sb("rope_a", [P, 2, S], F32, region))
        rope[0].ready = [SP.load(s_rope, lambda e: e.dma_start(rope[0].ap[:], consts["rope_a"]))]
        i_ready, a_ready = [free], []
        DVE(lambda e: e.memset(M[0][:], 0.0), free)
        mask_ready[0] = [DVE(lambda e: e.memset(M[0][0:64, 64:128], -BIG), DVE.last())]

        def evac_qi(o, b, m):
            q, a = copy_out(b, m)
            defer(1, lambda: rotate(q, a, 0, P, add_into(QI[:, o, :], i_ready)))
        DVE(lambda e: e.memset(top.ap[:], 0.0), free)
        gemm_fm("qi", X, 512, evac_qi, first=True)

        def evac_ki(o, b, m):
            q, a = copy_out(b, m, 72)
            bw = banks[6]

            def finish():
                for i in range(NT):
                    mt = PE(lambda e, i=i: e.transpose(bw.ap[:, 8 * i:8 * i + 8], q.ap[64:72, i * P:(i + 1) * P], ident[64:72, 64:72]), a, bw.free)
                w = DVE(lambda e: e.tensor_scalar(WI[:], bw.ap[:, 0:32].rearrange("p (i h) -> p i h", h=8),
                                                  8 ** -0.5 * 64 ** -0.5, None, ALU.mult), mt)
                bw.free = [w]
                i_ready.append(w)
                rotate(q, [a, mt], 0, 64, lambda x1, x2, rdy: ki_add(x1, x2, rdy))

            def ki_add(x1, x2, rdy):
                for half in range(2):
                    d = DVE(lambda e, half=half: e.tensor_tensor(KI[64 * half:64 * half + 64, :], x1.ap[0:64, :], x2.ap[0:64, :], ALU.add), rdy)
                i_ready.append(d)
                return d
            defer(1, finish)
        gemm_fm("ki", X, 72, evac_ki)

        def evac_qa(o, b, m):
            q, a = copy_out(b, m)
            defer(1, lambda: rotate(q, a, 0, P, add_into(Q[:, o, :], a_ready, POOL)))
            select_some(4.6)

        def select():
            for i in range(1, NT):
                w = (i + 1) * P
                s = SC[i - 1]
                for h in range(8):
                    b = banks[5 + h % 3]
                    o = 64 * (h % 2)
                    m = PE(lambda e, h=h, o=o, i=i, w=w: e.matmul(b.ap[:, 0:w], QI[o:o + 64, h // 2, i * P:(i + 1) * P], KI[o:o + 64, 0:w],
                                                         start=True, stop=True), i_ready, b.free)
                    q = scratch()
                    a = ACT(lambda e, q=q, w=w: e.activation(q.ap[:, 0:w], b.ap[:, 0:w], ACT_F.Relu), m, q.free)
                    b.free = [a]
                    if h == 0:
                        d = DVE(lambda e, q=q, i=i, h=h, w=w, s=s: e.tensor_scalar(s.ap[:, 0:w], q.ap[:, 0:w], WI[:, i, h:h + 1], None, ALU.mult), a, s.free)
                    else:
                        d = DVE(lambda e, q=q, i=i, h=h, w=w, s=s: e.scalar_tensor_tensor(
                            s.ap[:, 0:w], q.ap[:, 0:w], WI[:, i, h:h + 1], s.ap[:, 0:w], ALU.mult, ALU.add), a, d)
                    q.free = [d]
                    yield 0.25 + w / 1200
                d = DVE(lambda e, s=s, w=w: e.memset(s.ap[0:64, w - 64:w], SHUT), d)
                x1, x2 = s, SC2
                for _ in range(16):
                    d = DVE(lambda e, x1=x1, w=w: e.max(top.ap[:], x1.ap[:, 0:w]), d)
                    d = DVE(lambda e, x1=x1, x2=x2, w=w: e.match_replace(x2.ap[:, 0:w], top.ap[:], x1.ap[:, 0:w], USED), d)
                    x1, x2 = x2, x1
                    yield 0.26 + w / 426
                d = DVE(lambda e, i=i, w=w, x1=x1: e.tensor_scalar(M[i][:], x1.ap[:, 0:w], USED, -BIG, ALU.not_equal, ALU.mult), d, free)
                mask_ready[i] = [d]
                yield 0.3

        selecting = [None]

        def select_some(share=1e9, until=None):
            if selecting[0] is None:
                selecting[0] = select()
            while share > 0 and until not in mask_ready:
                cost = next(selecting[0], None)
                if cost is None:
                    return
                share -= cost
        gemm_fm("qa", X, 1024, evac_qa)

        def evac_ka(o, b, m):
            q, a = copy_out(b, m)
            defer(1, lambda: rotate(q, a, 0, P, add_twice([K2[2 * o], K2[2 * o + 1]], a_ready)))
            select_some(2.6)
        gemm_fm("ka", X, 256, evac_ka)

        def evac_va(i, at, k, b, m):
            a = ACT(lambda e: e.activation(V[:, i, at:at + k], b.ap[:, 0:k], ACT_F.Copy), m, free)
            b.free = [a]
            a_ready.append(a)
            select_some(2.6)
        gemm_tm("va", X, 256, evac_va)
        tick(force=True)
        select_some(until=2)
        attention(
            lambda h, i: Q[64 * (h % 2):64 * (h % 2) + 64, h // 2, i * P:(i + 1) * P],
            lambda h, w: K2[h // 4][64 * (h % 2):64 * (h % 2) + 64, 0:w],
            lambda h, j: V[:, j, 64 * (h // 4):64 * (h // 4) + 64],
            lambda i, w: M[i][:, 0:w], lambda i: (i + 1) * P, None, a_ready, X, PB, PT,
            [(0, 0), (0, 1), (0, 2), (1, 0), (1, 1), (1, 2), (0, 3), (1, 3)] + [(h, i) for h in range(2, 16) for i in range(NT)],
            lambda n: select_some(2.0) if n < 6 else select_some())
        gemm_fm("oa", X, 1024, lambda o, b, m: add_to_h(o, b, m))
        tick(force=True)
        end_of_a = phase_end()

    if STAGE >= 2:
        mean_square()
        normed(X, VEC["g_mlp0"], None, [v1_ready, h_ready])
        mlp("m0")
        tick(force=True)

    if STAGE >= 3:
        with ExitStack() as region:
            mean_square()
            free = phase_end()
            Q = sb("QB", [P, KC, S], F32, region)
            K = sb("KB", [P, KC, S], F32, region)
            V = sb("VB", [P, NT, D], F32, region)
            PB = [Buf(sb(f"PBB{i}", [P, S], F32, region), free) for i in range(5)]
            PT = [Buf(sb(f"PTB{i}", [P, NT, S], F32, region), free) for i in range(2)]
            tsum = sb("tsum", [P, S], F32, region)
            LF = sb("LF", [P, 4, NT * 16], F32, region)
            CK = sb("CK", [P, S], F32, region)
            CQ = sb("CQ", [P, S], F32, region)
            MH = [Buf(sb(f"MH{i}", [P, S], F32, region), free) for i in range(2)]
            mask_ready.clear()
            s_tsum = sem("tsum_in")
            tri = sb("tri", [P, S], F32, region)
            SP.load(s_tsum, lambda e: e.dma_start(tri[:], consts["tri"]), end_of_a)
            tsum_in = SP.load(s_tsum, lambda e: e.dma_start(tsum[:], consts["tsum"]), end_of_a)
            normed(X, VEC["g_kv"], None, [v1_ready, h_ready])
            POOL(lambda e: e.memset(CK[:], 0.0), free, POOL.last())
            for o in (32, 96):
                POOL(lambda e: e.memset(CK[o:o + 16, :], 1.0), POOL.last())
            POOL(lambda e: e.memset(CQ[:], 0.0), POOL.last())
            for o in (0, 64):
                c_set = POOL(lambda e: e.memset(CQ[o:o + 16, :], 1.0), POOL.last())
            POOL.wait([c_set])
            f_ready, b_ready = [], [free]

            def evac_f(i, at, k, b, m):
                d = DVE(lambda e: e.tensor_tensor(LF[:, 0, 16 * i:16 * i + 16], b.ap[:, 0:16], bf[:], ALU.add), m, free)
                b.free = [d]
                f_ready.append(d)
            def keep(dst):
                def evac(o, b, m):
                    a = ACT(lambda e: e.activation(dst[:, o, :], b.ap[:], ACT_F.Copy), m, free)
                    b.free = [a]
                    b_ready.append(a)
                return evac
            gemm_fm("kb", X, 1024, keep(K), first=True)
            gemm_tm("fb", X, 16, evac_f)
            d0 = DVE(lambda e: e.tensor_scalar(LF[:, 1, :], LF[:, 0, :], 0.0, None, ALU.min), f_ready)
            a = ACT(lambda e: e.activation(LF[:, 2, :], LF[:, 0, :], ACT_F.Abs), f_ready)
            a = ACT(lambda e: e.activation(LF[:, 3, :], LF[:, 2, :], ACT_F.Exp, scale=-1.0), a)
            d = DVE(lambda e: e.tensor_scalar(LF[:, 2, :], LF[:, 3, :], 1.0, None, ALU.add), a)
            a = ACT(lambda e: e.activation(LF[:, 3, :], LF[:, 2, :], ACT_F.Ln), d)
            d_lf = DVE(lambda e: e.tensor_tensor(LF[:, 0, :], LF[:, 1, :], LF[:, 3, :], ALU.subtract), a, d0)

            def running_sum():
                b = banks[6]
                for i in range(NT):
                    m = PE(lambda e, i=i: e.matmul(b.ap[0:16, P * i:S], LF[:, 0, 16 * i:16 * i + 16], tsum[:, 0:S - P * i],
                                                   start=(i == 0), stop=(i == NT - 1)), d_lf, tsum_in, b.free)
                for o in (32, 96):
                    a = ACT(lambda e: e.activation(CQ[o:o + 16, :], b.ap[0:16, :], ACT_F.Copy, scale=8.0), m, c_set)
                for o in (0, 64):
                    d = DVE(lambda e: e.tensor_scalar(CK[o:o + 16, :], b.ap[0:16, :], -8.0, None, ALU.mult), m, a)
                b.free = [d]
                b_ready.extend([a, d])
            defer(4, running_sum)


            def evac_vb(i, at, k, b, m):
                a = ACT(lambda e: e.activation(V[:, i, at:at + k], b.ap[:, 0:k], ACT_F.Copy), m, free)
                b.free = [a]
                b_ready.append(a)
            gemm_tm("vb", X, 1024, evac_vb)
            normed(X, VEC["g_attn_b"], None, [v1_ready, h_ready])
            gemm_fm("qb", X, 1024, keep(Q), first=True)
            tick(force=True)

            def decay(h, i, w):
                mh, o = MH[h % 2], 64 * (h % 2)
                if i == 0:
                    g = POOL(lambda e: e.tensor_scalar(mh.ap[:], CK[:], one_hot[:, h:h + 1], None, ALU.mult), b_ready, mh.free, c_ready)
                    mh.ready = [g]
                    mh.free = []
                return CQ[o:o + 48, i * P:(i + 1) * P], mh.ap[o:o + 48, 0:w], mh.ready

            def used_decay(h, m):
                MH[h % 2].free = [m]
            extra_hook[0] = used_decay
            attention(
                lambda h, i: Q[64 * (h % 2):64 * (h % 2) + 64, h // 2, i * P:(i + 1) * P],
                lambda h, w: K[64 * (h % 2):64 * (h % 2) + 64, h // 2, 0:w],
                lambda h, j: V[:, j, 64 * h:64 * h + 64],
                lambda i, w: tri[:, 384 - i * P:384 - i * P + w], lambda i: (i + 1) * P, decay, [b_ready, tsum_in], X, PB, PT)
            gemm_fm("ob", X, 1024, lambda o, b, m: add_to_h(o, b, m))
            tick(force=True)

    gm_ready = []

    def mod_gains(layer):
        for k, norm in ((0, "n1"), (1, "n2")):
            sc = MOD[layer][:, 8 + 24 * k:16 + 24 * k]
            d = DVE(lambda e, sc=sc, k=k, norm=norm: e.scalar_tensor_tensor(GM[:, 2 * layer + k, :], sc, 1.0, VEC[f"{norm}_{layer}"], ALU.add, ALU.mult),
                    mod_ready[layer], v1_ready)
        if layer == 0:
            d = DVE(lambda e: e.tensor_tensor(FG[:], GM[:, 0, :], VEC["g_final"], ALU.mult), d, v1_ready)
        gm_ready.append(d)

    def mod(layer, k):
        return MOD[layer][:, 8 * k:8 * k + 8]

    if STAGE >= 4:
        mean_square()
        normed(X, VEC["g_mlp1"], None, [v1_ready, h_ready])
        mlp("m1", at_end=lambda: (mod_gains(0), mod_gains(1)))
        tick(force=True)
        m, b = PE.last(), banks[6]
        a = ACT(lambda e: e.activation(rcol[:, 0:NT], b.ap[:, 0:NT], ACT_F.Sqrt, bias=eps[:, 0:1]), m)
        d = DVE(lambda e: e.reciprocal(rcol[:, NT:2 * NT], rcol[:, 0:NT]), a)
        d2 = DVE(lambda e: e.tensor_tensor(r2[:, 0:NT], b.ap[:, NT:2 * NT], rcol[:, NT:2 * NT], ALU.mult), d)
        b.free = [d2]
        d2 = DVE(lambda e: e.tensor_tensor(r2[:, 0:NT], r2[:, 0:NT], rcol[:, NT:2 * NT], ALU.mult), d2)
        a = ACT(lambda e: e.activation(r2[:, 0:NT], r2[:, 0:NT], ACT_F.Sqrt, bias=eps[:, 0:1]), d2)
        d2 = DVE(lambda e: e.reciprocal(r2[:, NT:2 * NT], r2[:, 0:NT]), a)
        d2 = DVE(lambda e: e.tensor_tensor(r2[:, 0:NT], r2[:, NT:2 * NT], rcol[:, NT:2 * NT], ALU.mult), d2)
        spread(d2, r2[:, 0:NT])
        z_rows = to_rows(banks[5], d, rcol[:, NT:2 * NT])

    if STAGE >= 5:
        normed(X, FG, mod(0, 0), [gm_ready, h_ready])
        for c in range(KC):
            d = DVE(lambda e, c=c: e.scalar_tensor_tensor(HT[:, c, :], HT[:, c, :], VEC["g_final"][:, c:c + 1], banks[5].ap[:], ALU.mult, ALU.mult),
                    z_rows, v1_ready, h_ready[c])
            h_ready[c] = [d]
        banks[5].free = [d]
        with ExitStack() as region:
            free = phase_end()
            rope[0] = Buf(sb("rope_b", [P, 2, S], F32, region))
            rope[0].ready = [SP.load(s_rope, lambda e: e.dma_start(rope[0].ap[:], consts["rope_b"]), free)]
            Q = sb("QC", [P, KC, S], F32, region)
            K2 = [sb(f"KC{i}", [P, S], F32, region) for i in range(4)]
            V = sb("VC", [P, NT, 256], F32, region)
            PB = [Buf(sb(f"PC{i}", [P, S], F32, region), free) for i in range(5)]
            PT = [Buf(sb(f"PTC{i}", [P, NT, S], F32, region), free) for i in range(2)]
            a_ready = [free]

            def head_norm(gain, done):
                def evac(o, b, m):
                    q, a = copy_out(b, m)

                    def norm():
                        r = scratch()
                        s = ACT(lambda e: e.activation(r.ap[:], q.ap[:], ACT_F.Square), a, r.free)
                        bm = banks[6]
                        mm = PE(lambda e: e.matmul(bm.ap[:], head_mean[:], r.ap[:], start=True, stop=True), s, bm.free)
                        s = ACT(lambda e: e.activation(r.ap[:], bm.ap[:], ACT_F.Sqrt, bias=eps[:, 0:1]), mm)
                        bm.free = [s]
                        d = DVE(lambda e: e.reciprocal(r.ap[:], r.ap[:]), s)
                        d = DVE(lambda e: e.scalar_tensor_tensor(q.ap[:], q.ap[:], gain, r.ap[:], ALU.mult, ALU.mult), d)
                        r.free = [d]
                        defer(2, lambda: rotate(q, d, 1, P, done(o)))
                    defer(1, norm)
                return evac
            gemm_fm("kc", X, 256, head_norm(VEC["kg"], lambda o: add_twice([K2[2 * o], K2[2 * o + 1]], a_ready)), first=True)

            def evac_vc(i, at, k, b, m):
                a = ACT(lambda e: e.activation(V[:, i, at:at + k], b.ap[:, 0:k], ACT_F.Copy), m, free)
                b.free = [a]
                a_ready.append(a)
            gemm_tm("vc", X, 256, evac_vc)
            gemm_fm("qc", X, 1024, head_norm(VEC["qg"], lambda o: add_into(Q[:, o, :], a_ready)))
            tick(force=True)
            attention(
                lambda h, i: Q[64 * (h % 2):64 * (h % 2) + 64, h // 2, i * P:(i + 1) * P],
                lambda h, w: K2[h // 4][64 * (h % 2):64 * (h % 2) + 64, 0:w],
                lambda h, j: V[:, j, 64 * (h // 4):64 * (h // 4) + 64],
                None, lambda i: S, None, a_ready, X, PB, PT)
            gemm_fm("oc", X, 1024, lambda o, b, m: add_to_h(o, b, m, mod(0, 2)))
            tick(force=True)
    if STAGE >= 6:
        mean_square()
        normed(X, GM[:, 1, :], mod(0, 3), [gm_ready, h_ready])
        mlp("m2", mod(0, 5))
        tick(force=True)
    if STAGE >= 7:
        mean_square()
        normed(X, GM[:, 2, :], mod(1, 0), [gm_ready, h_ready])
        with ExitStack() as region:
            free = phase_end()
            VT = sb("VT", [P, NT, 3072], F32, region)
            wsT = sb("wsT", [P, 16, P], F32, region)
            bs = sb("bs", [16, P], F32, region)
            s_g = sem("gmlp_in")
            with ExitStack() as sub:
                row_a = Buf(sb("row_a", [P, 3072], F32, sub))
                row_b = Buf(sb("row_b", [P, 3072], F32, sub))
                s_a, s_b = sem("row_a_in"), sem("row_b_in")
                row_a.ready = [SP.load(s_a, lambda e: e.dma_start(row_a.ap[:], t["gmlp_b_in_2"][0, 3072:6144].partition_broadcast(P)), free)]
                row_b.ready = [SP.load(s_b, lambda e: e.dma_start(row_b.ap[:], t["gmlp_ln_g_2"][0].partition_broadcast(P)), free)]
                bs_in = SP.load(s_g, lambda e: e.dma_start(bs[:], t["gmlp_b_s_2"][0]), free)
                s_w = [sem(f"ws_in{i}") for i in range(2)]
                turned = []

                def turn_ws(k):
                    w = tmp[k % 2]
                    ld = SP.load(s_w[k % 2], lambda e: e.dma_start(
                        w.ap[:].rearrange("p (g q) -> p g q", q=P),
                        t["gmlp_w_s_2"][0, 4 * k:4 * k + 4].rearrange("g p q -> p g q")), w.free)

                    def turn_now():
                        b = banks[4 + k % 2]
                        for g in range(4):
                            m = PE(lambda e: e.transpose(b.ap[:, g * P:(g + 1) * P], w.ap[:, g * P:(g + 1) * P], ident[:]), ld, b.free)
                        w.free = [m]
                        d = DVE(lambda e: e.tensor_copy(wsT[:, 4 * k:4 * k + 4, :].rearrange("p g q -> p (g q)"), b.ap[:]), m, free)
                        b.free = [d]
                        turned.append(d)
                    defer(6, turn_now)
                for k in range(4):
                    defer(4 + 8 * k, lambda k=k: turn_ws(k))
                v_ready = [[] for _ in range(NT)]

                def evac_gv(i, at, k, b, m):
                    d = DVE(lambda e: e.tensor_tensor(VT[:, i, at:at + k], b.ap[:, 0:k], row_a.ap[:, at:at + k], ALU.add), m, row_a.ready)
                    b.free = [d]
                    a = ACT(lambda e: e.activation(VT[:, i, at:at + k], VT[:, i, at:at + k], ACT_F.Gelu), d)
                    v_ready[i].append(a)
                    if at % 512:
                        s = DVE(lambda e, f=at // 512: e.bn_stats(bst[:, i, f, :], VT[:, i, 512 * f:512 * f + 512]), v_ready[i])
                        v_ready[i] = [s]
                gemm_tm("gv", X, 3072, evac_gv)
                row_a.ready = [SP.load(s_a, lambda e: e.dma_start(row_a.ap[:], t["gmlp_ln_b_2"][0].partition_broadcast(P)), DVE.last())]
                for i in range(NT):
                    d = DVE(lambda e, i=i: e.bn_aggr(mv[:, i, :], bst[:, i, :, :]), v_ready[i])
                a = ACT(lambda e: e.activation(rsv[:], mv[:, :, 1], ACT_F.Sqrt, bias=eps[:, 0:1]), d)
                d = DVE(lambda e: e.reciprocal(rsv[:], rsv[:]), a)
                d = DVE(lambda e: e.scalar_tensor_tensor(nmr[:], mv[:, :, 0], -1.0, rsv[:], ALU.mult, ALU.mult), d)
                vn = []
                for f in range(6):
                    for i in range(NT):
                        z = VT[:, i, 512 * f:512 * f + 512]
                        a = ACT(lambda e: e.activation(z, z, ACT_F.Identity, bias=nmr[:, i:i + 1], scale=rsv[:, i:i + 1]), d)
                        d2 = DVE(lambda e, z=z, f=f: e.tensor_tensor(z, z, row_b.ap[:, 512 * f:512 * f + 512], ALU.mult), a, row_b.ready)
                        g = (DVE if i == 3 else POOL)(lambda e, z=z, f=f: e.tensor_tensor(z, z, row_a.ap[:, 512 * f:512 * f + 512], ALU.add), d2, row_a.ready)
                        vn.append(g)
            free = phase_end()
            Y = Split(sb("Yhi", [P, KC, S], F32R, region), sb("Ylo", [P, KC, S], F32R, region), free)

            def mix(j, q, a, write_after):
                b = banks[4 + j % 2]
                parts = [(0, P, (P * j) // 192)] if (P * j) // 192 == (P * j + P - 1) // 192 else [
                    (0, 64, (P * j) // 192), (64, 64, (P * j + 64) // 192)]
                n = 0
                for o, rows, g in parts:
                    PE(lambda e, o=o, rows=rows, g=g: e.matmul(
                        b.ap[o:o + rows, :].rearrange("r (i q) -> r i q", q=P),
                        ident[0:16, g:g + 1].to_broadcast([16, rows]), bs[:].unsqueeze(1).to_broadcast([16, NT, P]),
                        start=True, stop=False, skip_group_check=True), b.free, bs_in, vn[NT * (j // 4):NT * (j // 4) + NT], turned)
                    for i in range(NT):
                        m = PE(lambda e, o=o, rows=rows, g=g, i=i: e.matmul(
                            b.ap[o:o + rows, i * P:(i + 1) * P], VT[:, i, P * j + o:P * j + o + rows], wsT[:, g, :],
                            start=False, stop=(i == NT - 1), skip_group_check=True))
                d = DVE(lambda e: e.tensor_tensor(q.ap[:], b.ap[:], q.ap[:], ALU.mult), m, a)
                b.free = [d]
                c = j % 8
                a2 = ACT(lambda e: e.activation(Y.hi[:, c, :], q.ap[:], ACT_F.Copy), d, write_after)
                d = DVE(lambda e: e.tensor_tensor(Y.lo[:, c, :], q.ap[:], Y.hi[:, c, :].bitcast(F32), ALU.subtract), a2)
                q.free = [d]
                Y.ready[c] = [a2, d]
            for g in range(3):
                write_after = list(Y.free)

                def evac_gu(o, b, m, g=g, write_after=write_after):
                    q = hold()
                    j = 8 * g + o
                    a = ACT(lambda e: e.activation(q.ap[:], b.ap[:], ACT_F.Gelu, bias=VEC["b_in"][:, j:j + 1]), m, q.free)
                    b.free = [a]
                    defer(2, lambda: mix(j, q, a, write_after))
                gemm_fm("gu", X, 1024, evac_gu)
                tick(force=True)
                gemm_fm("go", Y, 1024, lambda o, b, m: add_to_h(o, b, m, mod(1, 2), last=(g == 2)))
                tick(force=True)
    if STAGE >= 8:
        mean_square()
        normed(X, GM[:, 3, :], mod(1, 3), [gm_ready, h_ready])
        mlp("m3", mod(1, 5))
        tick(force=True)

    s_out = sem("out_done")
    with ExitStack() as region:
        free = phase_end()
        O = sb("O", [P, NT, D], F32, region)
        for i in range(NT):
            vs = []
            for half in range(2):
                b = gemm_bank()
                for c in range(4):
                    cc = 4 * half + c
                    m = PE(lambda e, c=c, cc=cc, i=i, b=b: e.transpose(b.ap[:, c * P:(c + 1) * P], HT[:, cc, i * P:(i + 1) * P], ident[:]), h_ready[cc], b.free)
                dst = O[:, i, 512 * half:512 * half + 512]
                if half:
                    v = DVE(lambda e, dst=dst, b=b: e.tensor_copy(dst, b.ap[:]), m, free)
                else:
                    v = ACT(lambda e, dst=dst, b=b: e.activation(dst, b.ap[:], ACT_F.Copy), m, free)
                b.free = [v]
                vs.append(v)
            o_done = SP.load(s_out, lambda e, i=i: e.dma_start(out[0, i * P:(i + 1) * P, :], O[:, i, :]), vs)
    SP.wait([o_done])


def shape_constants():
    f = np.float32
    i = np.arange(P)
    inv = (1.0 / (f(10000.0) ** (np.arange(0, 64, 2, dtype=f) / f(64)))).astype(f)
    ang = np.arange(S, dtype=f)[:, None] * inv[None, :]
    c, s = np.cos(ang).T.astype(f), np.sin(ang).T.astype(f)
    rope_a = np.stack([np.tile(c, (4, 1)), np.concatenate([-s, s, -s, s])], 1)
    perm_half = np.zeros((P, P), f)
    perm_half[i, i ^ 32] = 1
    perm_pair = np.zeros((P, P), f)
    perm_pair[i, i ^ 1] = 1
    tok = np.arange(S)
    row = (tok // 64 - (S // 64) // 2).astype(f)
    col = (tok % 64 - 32).astype(f)
    freq = (f(10000.0) ** (-np.arange(16, dtype=f) / f(16))).astype(f)
    ang = np.concatenate([row[:, None] * freq, col[:, None] * freq], -1)
    c, s = np.cos(ang).T.astype(f), np.sin(ang).T.astype(f)
    sign = np.where(i % 2, 1.0, -1.0).astype(f)[:, None]
    rope_b = np.stack([c[(i % 64) // 2], sign * s[(i % 64) // 2]], 1)
    tri = np.zeros((P, S), f)
    tri[:, 384:] = np.where(i[None, :] > i[:, None], -BIG, 0.0)
    tsum = np.ones((P, S), f)
    tsum[:, 0:P] = i[:, None] <= i[None, :]
    one_hot = np.tile(np.eye(32, 16, dtype=f), (4, 1))
    return {
        "ident": np.eye(P, dtype=f), "head_mean": np.kron(np.eye(2), np.full((64, 64), 1 / 64)).astype(f),
        "perm_half": perm_half, "perm_pair": perm_pair, "one_hot": one_hot,
        "rope_a": rope_a.astype(f), "rope_b": rope_b.astype(f), "tri": tri, "tsum": tsum,
    }


def kernel(**inputs):
    import numpy as _np
    import concourse.bacc as _bacc
    from concourse import mybir as _mybir
    from concourse.bass_utils import run_bass_kernel_spmd as _run

    nc = _bacc.Bacc("TRN2", target_bir_lowering=False, num_devices=1)
    arrays, t, consts = {}, {}, {}
    for name in inputs:
        a = _np.ascontiguousarray(inputs[name])
        arrays[f"in_{name}"] = a
        t[name] = nc.dram_tensor(f"in_{name}", a.shape, _mybir.dt.from_np(a.dtype), kind="ExternalInput").ap()
    for name, a in shape_constants().items():
        a = _np.ascontiguousarray(a)
        arrays[f"const_{name}"] = a
        consts[name] = nc.dram_tensor(f"const_{name}", a.shape, _mybir.dt.from_np(a.dtype), kind="ExternalInput").ap()
    out = nc.dram_tensor("out_0", (1, S, D), F32, kind="ExternalOutput").ap()
    program(nc, t, consts, out)
    r = _run(nc, [arrays], core_ids=[0])
    return r.results[0]["out_0"]
```

```python
from contextlib import ExitStack

import numpy as np

import concourse.bass as bass
from concourse import mybir

ALU = mybir.AluOpType
ACT_F = mybir.ActivationFunctionType
F32 = mybir.dt.float32
F32R = mybir.dt.float32r

P = 128
S = 512
D = 1024
NT = S // P
KC = D // P
UC = 256
EPS = 1e-6
BIG = 1e30
USED = -3e38
SHUT = -1e38


class Engine:

    def __init__(self, sem):
        self.sem, self.count, self.seen, self.eng = sem, 0, {}, None

    def wait(self, waits):
        for sem, value in flat(waits):
            if self.seen.get(sem.name, 0) < value:
                self.seen[sem.name] = value
                self.eng.wait_ge(sem, value)

    def __call__(self, issue, *waits, inc=True):
        self.wait(waits)
        done = issue(self.eng)
        if not inc:
            return None
        done.then_inc(self.sem, 1)
        self.count += 1
        return (self.sem, self.count)

    def last(self):
        return (self.sem, self.count)


class Loader(Engine):

    def __init__(self):
        self.at, self.seen, self.eng = {}, {}, None

    def load(self, sem, issue, *waits):
        self.wait(waits)
        issue(self.eng).then_inc(sem, 16)
        self.at[sem.name] = self.at.get(sem.name, 0) + 16
        return (sem, self.at[sem.name])


def flat(waits):
    for w in waits:
        if w is None:
            continue
        if isinstance(w, tuple) and len(w) == 2 and isinstance(w[1], int):
            yield w
        else:
            yield from flat(w)


class Buf:

    def __init__(self, ap, free=()):
        self.ap, self.ready, self.free = ap, [], list(free)


class Split:

    def __init__(self, hi, lo, free=()):
        self.hi, self.lo = hi, lo
        self.ready = [[] for _ in range(KC)]
        self.free = list(free)


def program(nc, t, consts, out):
    with ExitStack() as ctx:
        PE, ACT, DVE, POOL = (Engine(ctx.enter_context(nc.semaphore(n))) for n in ("pe", "act", "dve", "pool"))
        SP = Loader()
        for engine, issuer in ((PE, nc.tensor), (ACT, nc.scalar), (DVE, nc.vector), (POOL, nc.gpsimd), (SP, nc.sync)):
            engine.eng = issuer
        body(nc, ctx, t, consts, out, PE, ACT, DVE, POOL, SP)


def body(nc, ctx, t, consts, out, PE, ACT, DVE, POOL, SP):
    def sem(name):
        return ctx.enter_context(nc.semaphore(name))

    def sb(name, shape, dt=F32, stack=ctx):
        return stack.enter_context(nc.sbuf_tensor(name, shape, dt))

    banks = [Buf(ctx.enter_context(nc.psum_tensor(f"bank{i}", [P, 512], F32))) for i in range(8)]

    HT = sb("HT", [P, KC, S])
    h_ready = [[] for _ in range(KC)]
    X = Split(sb("Xhi", [P, KC, S], F32R), sb("Xlo", [P, KC, S], F32R))
    NRAW, NSP = 2, 2
    raw = [Buf(sb(f"raw{i}", [P, KC, UC])) for i in range(NRAW)]
    raw_sem = [sem(f"raw_in{i}") for i in range(NRAW)]
    whi = [sb(f"whi{i}", [P, KC, UC], F32R) for i in range(NSP)]
    wlo = [sb(f"wlo{i}", [P, KC, UC], F32R) for i in range(NSP)]
    wfree = [[] for _ in range(NSP)]
    tmp = [Buf(sb(f"tmp{i}", [P, S])) for i in range(4)]
    held = [Buf(sb(f"held{i}", [P, S])) for i in range(3)]
    rstd = Buf(sb("rstd", [P, S]))
    rope = [None]
    ident = sb("ident", [P, P])
    ones = sb("ones", [P, P])
    mean = sb("mean", [P, 1])
    rcol = sb("rcol", [P, 2 * NT])
    r2 = sb("r2", [P, 2 * NT])
    FG = sb("FG", [P, KC])
    head_mean = sb("head_mean", [P, P])
    perm = [sb(f"perm{i}", [P, P]) for i in range(2)]
    one_hot = sb("one_hot", [P, 16])
    eps = sb("eps", [P, 1])
    warm = sb("warm", [P, 1])
    V1 = sb("V1", [P, 114])
    V2 = sb("V2", [P, 96])
    bf = sb("bf", [P, 16])
    cond = sb("cond", [P, 3, KC])
    MOD = [sb(f"MOD{i}", [P, 48]) for i in range(2)]
    GM = sb("GM", [P, 4, KC])
    acc = [Buf(sb(f"acc{i}", [P, UC])) for i in range(2)]
    stats = sb("stats", [P, 6, 4])
    stat = [Buf(stats[:, i, :]) for i in range(6)]
    bst = sb("bst", [P, NT, 6, 6])
    mv = sb("mv", [P, NT, 2])
    rsv = sb("rsv", [P, NT])
    nmr = sb("nmr", [P, NT])

    tmp_at = [0]

    def scratch():
        b = tmp[tmp_at[0] % len(tmp)]
        tmp_at[0] += 1
        return b

    held_at = [0]

    def hold():
        b = held[held_at[0] % len(held)]
        held_at[0] += 1
        return b

    later = []

    def defer(n, fn):
        later.append([n, fn])

    def tick(force=False):
        for item in later:
            item[0] -= 1
        while True:
            due = [item for item in later if force or item[0] <= 0]
            if not due:
                return
            later.remove(due[0])
            due[0][1]()

    s_const = sem("const_in")

    def const(dst, name):
        src = consts[name]
        return SP.load(s_const, lambda e, dst=dst, src=src: e.dma_start(dst, src))

    s_ident = sem("ident_in")
    i_in = SP.load(s_ident, lambda e: e.dma_start(ident[:], consts["ident"]))
    DVE(lambda e: e.memset(mean[:], 1.0 / D))
    DVE(lambda e: e.memset(ones[:], 1.0))
    d_const = DVE(lambda e: e.memset(eps[:], EPS))
    s_vec = sem("vec_in")

    def phase_end():
        return [PE.last(), ACT.last(), DVE.last(), POOL.last()]

    def block_of(w, r0, c0, n):
        return w[r0:r0 + D, c0:c0 + n].rearrange("(c p) n -> p c n", p=P)

    plan = []

    def plan_cols(name, w, c0, n, r0=0):
        for c in range(c0, c0 + n, UC):
            k = min(UC, c0 + n - c)
            plan.append((name, block_of(w, r0, c, k), k))

    ada = [("ada", block_of(t["ada_w_2"][i], 0, c, UC), (i, c // P)) for i in range(2) for c in range(0, 6 * D, UC)]

    def plan_mlp(name, up, down, with_ada):
        start = len(plan)

        def up_g(g):
            plan_cols(name + "u", up, g * D, D)

        def down_g(g):
            plan_cols(name + "d", down, 0, D, r0=g * D)
        for f, g in ((up_g, 0), (up_g, 1), (down_g, 0), (up_g, 2), (down_g, 1), (up_g, 3), (down_g, 2), (down_g, 3)):
            f(g)
        if with_ada:
            units = plan[start:]
            del plan[start:]
            for i, u in enumerate(units):
                plan.append(u)
                if 1 <= i < 25:
                    plan.append(ada.pop(0))

    wa = t["w_in_a"][0]
    plan_cols("qi", wa, 1536, 256)
    plan_cols("ki", wa, 2048, 72)
    plan_cols("qj", wa, 1792, 256)
    plan_cols("qa", wa, 0, 1024)
    plan_cols("ka", wa, 1024, 256)
    plan_cols("va", wa, 1280, 256)
    plan_cols("oa", t["w_o_a"][0], 0, 1024)
    plan_mlp("m0", t["w_up"][0], t["w_down"][0], True)
    wk = t["w_kv_b"]
    plan_cols("kb", wk, 0, 1024)
    plan_cols("fb", wk, 2048, 16)
    plan_cols("vb", wk, 1024, 1024)
    plan_cols("qb", t["w_q_b"][0], 0, 1024)
    plan_cols("ob", t["w_o_b"][0], 0, 1024)
    plan_mlp("m1", t["w_up"][1], t["w_down"][1], True)
    wq = t["attn_w_qkv_2"][0]
    plan_cols("kc", wq, 1024, 256)
    plan_cols("qc", wq, 0, 1024)
    plan_cols("vc", wq, 1280, 256)
    plan_cols("oc", t["attn_w_o_2"][0], 0, 1024)
    plan_mlp("m2", t["mlp_w_in_2"][0], t["mlp_w_out_2"][0], False)
    wg = t["gmlp_w_in_2"][0]
    plan_cols("gv", wg, 3072, 3072)
    for g in range(3):
        plan_cols("gu", wg, g * D, D)
        plan_cols("go", t["gmlp_w_out_2"][0], 0, D, r0=g * D)
    plan_mlp("m3", t["mlp_w_in_2"][1], t["mlp_w_out_2"][1], False)

    loaded, split_at, used = [0], [0], [0]
    loads, splits = {}, {}
    mod_ready = [[], []]
    v2_ready = []
    cond_ready = []

    def load_next():
        n = loaded[0]
        if n >= len(plan):
            return
        name, src, k = plan[n]
        k = UC if name == "ada" else k
        place = raw[n % NRAW]
        loads[n] = SP.load(raw_sem[n % NRAW], lambda e, place=place, src=src, k=k: e.dma_start(place.ap[:, :, 0:k], src), place.free)
        place.free = []
        loaded[0] += 1

    gemm_no = [0]

    def split_next():
        while split_at[0] < len(plan):
            n = split_at[0]
            split_at[0] += 1
            if n >= loaded[0]:
                load_next()
            name, _, k = plan[n]
            place = raw[n % NRAW]
            if name == "ada":
                ada_unit(place, loads[n], *k)
                load_next()
                continue
            slot = gemm_no[0] % NSP
            gemm_no[0] += 1
            hi, lo = whi[slot], wlo[slot]
            ready = []
            for c0, c1 in ((0, KC // 2), (KC // 2, KC)):
                a = ACT(lambda e: e.activation(hi[:, c0:c1, 0:k], place.ap[:, c0:c1, 0:k], ACT_F.Copy), loads[n], wfree[slot])
                p = POOL(lambda e: e.tensor_tensor(
                    lo[:, c0:c1, 0:k], place.ap[:, c0:c1, 0:k], hi[:, c0:c1, 0:k].bitcast(F32), ALU.subtract), a, wfree[slot])
                ready += [[a, p]] * (KC // 2)
            place.free = [p]
            splits[n] = (name, slot, ready)
            load_next()
            return

    def ada_unit(place, arrived, layer, col):
        a = acc[(col // 2) % 2]
        cd = cond[:, 2, :]
        tok = DVE(lambda e: e.tensor_scalar(a.ap[:], place.ap[:, 0, :], cd[:, 0:1], None, ALU.mult), arrived, cond_ready, a.free)
        for c in range(1, KC):
            tok = DVE(lambda e, c=c: e.scalar_tensor_tensor(a.ap[:], place.ap[:, c, :], cd[:, c:c + 1], a.ap[:], ALU.mult, ALU.add), tok)
        place.free = [tok]
        a.ready = [tok]

        def sums():
            b = banks[7]
            for j in range(2):
                m = PE(lambda e, j=j: e.matmul(b.ap[:, j:j + 1], a.ap[:, j * P:(j + 1) * P], ones[:, 0:1], start=True, stop=True),
                       a.ready, b.free)
            a.free = [m]
            d = DVE(lambda e: e.tensor_tensor(MOD[layer][:, col:col + 2], b.ap[:, 0:2],
                                              V2[:, layer * 48 + col:layer * 48 + col + 2], ALU.add), m, v2_ready)
            b.free = [d]
            mod_ready[layer] = [d]
        defer(3, sums)

    def unit(name):
        while used[0] not in splits:
            if plan[used[0]][0] == "ada" and used[0] < split_at[0]:
                used[0] += 1
                continue
            split_next()
        n = used[0]
        used[0] += 1
        got, slot, ready = splits.pop(n)
        assert got == name, (got, name)
        return slot, ready

    gb = [0]

    def gemm_bank():
        b = banks[gb[0] % 4]
        gb[0] += 1
        return b

    def gemm_fm(name, x, n_cols, evac, first=False):
        at = 0
        if first:
            gemm_fm_first(name, x, evac)
            at = UC
        while at < n_cols:
            slot, ready = unit(name)
            split_next()
            k = min(UC, n_cols - at)
            for j in range(0, k, P):
                m_cols = min(P, k - j)
                b = gemm_bank()
                n = 0
                for c in range(KC):
                    for w, v in ((whi, x.hi), (whi, x.lo), (wlo, x.hi)):
                        m = PE(lambda e, w=w, v=v, c=c, j=j, n=n, b=b, m_cols=m_cols: e.matmul(
                            b.ap[0:m_cols, :], w[slot][:, c, j:j + m_cols], v[:, c, :], start=(n == 0), stop=(n == 3 * KC - 1)),
                            ready[c], b.free, x.ready[c], inc=(n == 3 * KC - 1))
                        n += 1
                x.free = [m]
                wfree[slot] = [m]
                tick()
                evac((at + j) // P, b, m)
            at += k

    def gemm_fm_first(name, x, evac):
        slot, ready = unit(name)
        split_next()
        pair = [gemm_bank(), gemm_bank()]
        for c in range(KC):
            for j, b in enumerate(pair):
                for n, (w, v) in enumerate(((whi, x.hi), (whi, x.lo), (wlo, x.hi))):
                    m = PE(lambda e: e.matmul(b.ap[:], w[slot][:, c, j * P:(j + 1) * P], v[:, c, :],
                                              start=(c == 0 and n == 0), stop=(c == KC - 1 and n == 2)),
                           ready[c], b.free, x.ready[c], inc=(c == KC - 1 and n == 2))
                    if m:
                        b.ready = [m]
        x.free = [m]
        wfree[slot] = [m]
        for j, b in enumerate(pair):
            tick()
            evac(j, b, b.ready)

    def gemm_tm(name, x, n_cols, evac):
        at = 0
        while at < n_cols:
            slot, ready = unit(name)
            split_next()
            k = min(UC, n_cols - at)
            for i in range(NT):
                b = gemm_bank()
                n = 0
                for c in range(KC):
                    for v, w in ((x.hi, whi), (x.hi, wlo), (x.lo, whi)):
                        m = PE(lambda e, w=w, v=v, c=c, i=i, n=n, b=b, k=k: e.matmul(
                            b.ap[:, 0:k], v[:, c, i * P:(i + 1) * P], w[slot][:, c, 0:k], start=(n == 0), stop=(n == 3 * KC - 1)),
                            ready[c], b.free, x.ready[c], inc=(n == 3 * KC - 1))
                        n += 1
                x.free = [m]
                wfree[slot] = [m]
                tick()
                evac(i, at, k, b, m)
            at += k

    gained = [None]

    def square(c, gain=None):
        if c == KC - 2:
            ACT(lambda e: e.activation(warm[:], eps[:], ACT_F.Sqrt), d_const)
        for total, at, g in [(rstd, 0, None)] + ([(gained[0], NT, gain)] if gain is not None else []):
            scale = 1.0 if g is None else g[:, c:c + 1]
            q = total if c == 0 else hold()
            q.ready = [ACT(lambda e: e.activation(q.ap[:], HT[:, c, :], ACT_F.Square, scale=scale), h_ready[c], q.free)]
            if 0 < c < KC - 1:
                d = DVE(lambda e: e.tensor_tensor(total.ap[:], total.ap[:], q.ap[:], ALU.add), q.ready, total.ready)
                q.free = [d]
                total.ready = [d]

            def sums(src, first, at):
                b = banks[6]
                for i in range(NT):
                    m = PE(lambda e: e.matmul(b.ap[:, at + i:at + i + 1], src.ap[:, i * P:(i + 1) * P], mean[:],
                                              start=(first and at == 0 and i == 0), stop=(not first and i == NT - 1), skip_group_check=True),
                           src.ready, b.free, d_const)
                src.free = [m]
            if c == KC - 2:
                defer(1, lambda total=total, at=at: sums(total, True, at))
            elif c == KC - 1:
                defer(1, lambda q=q, at=at: sums(q, False, at))

    def mean_square():
        tick(force=True)
        m = PE.last()
        a = ACT(lambda e: e.activation(rcol[:, 0:NT], banks[6].ap[:, 0:NT], ACT_F.Sqrt, bias=eps[:, 0:1]), m)
        banks[6].free = [a]
        spread(DVE(lambda e: e.reciprocal(rcol[:, NT:2 * NT], rcol[:, 0:NT]), a), rcol[:, NT:2 * NT])

    def to_rows(b, ready, col):
        for i in range(NT):
            m = PE(lambda e: e.matmul(b.ap[:, i * P:(i + 1) * P], col[:, i:i + 1].to_broadcast([P, P]), ident[:],
                                      start=True, stop=True), ready, i_in, b.free)
        return m

    def keep_rows():
        a = ACT(lambda e: e.activation(rstd.ap[:], rows.ap[:], ACT_F.Copy), rows.ready, rows.free, rstd.free)
        banks[6].free = [a]
        rstd.ready = [a]

    rows = banks[6]

    def spread(ready, col):
        b = banks[6]
        m = to_rows(b, ready, col)
        rows.ready = [m]

    def normed(x, gain, shift, ready, r=banks[6]):
        def first(c):
            q = scratch()
            d = DVE(lambda e: e.scalar_tensor_tensor(q.ap[:], HT[:, c, :], gain[:, c:c + 1], r.ap[:], ALU.mult, ALU.mult),
                    r.ready, ready, q.free)
            r.free = [d]
            if shift is None:
                a = ACT(lambda e: e.activation(x.hi[:, c, :], q.ap[:], ACT_F.Copy), d, x.free)
            else:
                a = ACT(lambda e: e.activation(x.hi[:, c, :], q.ap[:], ACT_F.Identity, bias=shift[:, c:c + 1]), d, x.free)
            q.free = [a]
            return c, q, d, a

        def second(c, q, d, a):
            hi, lo = x.hi[:, c, :].bitcast(F32), x.lo[:, c, :]
            if shift is not None:
                p = DVE(lambda e: e.scalar_tensor_tensor(lo, q.ap[:], shift[:, c:c + 1], hi, ALU.add, ALU.subtract), a)
            elif c % 3 == 1:
                p = POOL(lambda e: e.tensor_tensor(lo, q.ap[:], hi, ALU.subtract), d, a)
            else:
                p = DVE(lambda e: e.tensor_tensor(lo, q.ap[:], hi, ALU.subtract), a)
            q.free = [p]
            x.ready[c] = [a, p]
        behind = None
        for c in range(KC):
            now = first(c)
            if behind:
                second(*behind)
            behind = now
        second(*behind)

    def add_to_h(o, b, m, gate=None, ready=(), last=True):
        if gate is None:
            d = DVE(lambda e: e.tensor_tensor(HT[:, o, :], b.ap[:], HT[:, o, :], ALU.add), m, h_ready[o])
        else:
            d = DVE(lambda e: e.scalar_tensor_tensor(HT[:, o, :], b.ap[:], gate[:, o:o + 1], HT[:, o, :], ALU.mult, ALU.add), m, h_ready[o], ready)
        b.free = [d]
        h_ready[o] = [d]
        if last:
            square(o, VEC["g_final"] if last == "final" else None)

    def mlp(name, gate=None, ready=(), at_end=lambda: None):
        with ExitStack() as region:
            free = phase_end()
            if name == "m1":
                gained[0] = Buf(sb("gained", [P, S], F32, region), free)
            H = [Split(sb(f"{name}Hhi{i}", [P, KC, S], F32R, region), sb(f"{name}Hlo{i}", [P, KC, S], F32R, region), free) for i in range(2)]

            def up(g):
                h = H[g % 2]
                write_after = list(h.free)

                def evac(o, b, m):
                    q, r = scratch(), scratch()
                    a = ACT(lambda e: e.activation(q.ap[:], b.ap[:], ACT_F.Relu), m, q.free)
                    b.free = [a]
                    a2 = ACT(lambda e: e.activation(h.hi[:, o, :], q.ap[:], ACT_F.Square), a, write_after)
                    d = DVE(lambda e: e.tensor_tensor(r.ap[:], q.ap[:], q.ap[:], ALU.mult), a, r.free)
                    q.free = [a2, d]
                    d = DVE(lambda e: e.tensor_tensor(h.lo[:, o, :], r.ap[:], h.hi[:, o, :].bitcast(F32), ALU.subtract), a2, d, write_after)
                    r.free = [d]
                    h.ready[o] = [a2, d]
                gemm_fm(name + "u", X, D, evac, first=(g == 0))

            def down(g):
                gemm_fm(name + "d", H[g % 2], D, lambda o, b, m: add_to_h(o, b, m, gate, ready, g == 3 and {"m1": "final", "m3": False}.get(name, True)))
            for f, g in ((up, 0), (up, 1), (down, 0), (up, 2), (down, 1), (up, 3), (down, 2), (down, 3)):
                if (f, g) == (down, 3):
                    at_end()
                f(g)

    rb = [0]

    def rotate(src, ready, p, rows, done, other=POOL):
        b, CS = banks[4], rope[0]
        rb[0] += 1
        m = PE(lambda e: e.matmul(b.ap[0:rows, :], perm[p][0:rows, 0:rows], src.ap[0:rows, :], start=True, stop=True), ready, b.free, c_ready)
        r = scratch()
        d = DVE(lambda e: e.tensor_tensor(r.ap[0:rows, :], b.ap[0:rows, :], CS.ap[0:rows, 1, :], ALU.mult), m, r.free, CS.ready)
        b.free = [d]
        q = other(lambda e: e.tensor_tensor(src.ap[0:rows, :], src.ap[0:rows, :], CS.ap[0:rows, 0, :], ALU.mult), m, ready, CS.ready)
        d = done(src, r, [d, q])
        src.free, r.free = [d], [d]

    def add_into(dst, ready_list, on=None):
        def done(x1, x2, ready):
            d = (on or DVE)(lambda e: e.tensor_tensor(dst, x1.ap[:], x2.ap[:], ALU.add), ready)
            ready_list.append(d)
            return d
        return done

    def add_twice(dsts, ready_list):
        def done(x1, x2, ready):
            for i, dst in enumerate(dsts):
                d = DVE(lambda e, i=i, dst=dst: e.tensor_tensor(
                    dst[0:64, :], x1.ap[64 * i:64 * i + 64, :], x2.ap[64 * i:64 * i + 64, :], ALU.add), ready)

            def copies():
                for dst in dsts:
                    a = ACT(lambda e: e.activation(dst[64:128, :], dst[0:64, :], ACT_F.Copy), d)
                ready_list.extend([d, a])
            defer(1, copies)
            return d
        return done

    def copy_out(b, m, rows=P):
        q = hold()
        a = ACT(lambda e: e.activation(q.ap[0:rows, :], b.ap[0:rows, :], ACT_F.Copy), m, q.free)
        b.free = [a]
        return q, a

    LAG = 4
    mask_ready = {}

    def attention(heads_q, heads_k, heads_v, mask, width, extra, ready, x, PB, PT, steps=None, between=None):
        scale = 0.125
        steps = steps or [(h, i) for h in range(16) for i in range(NT)]
        first_of = [steps.index((h, 0)) for h in range(16)] + [len(steps) + 8] * 2
        last_of = [max(n for n, s in enumerate(steps) if s[0] == h) for h in range(16)]
        values_at = {}
        for h in range(16):
            for j in range(NT):
                values_at.setdefault(LAG + min(last_of[h] + min(2 + j, 4), first_of[h + 2] - 1), []).append((h, j))
        prob = {}
        write_after = list(x.free)

        def scores(n):
            h, i = steps[n]
            w = width(i)
            b, pb, st = banks[n % 3], PB[n % len(PB)], stat[n % len(stat)]
            q, k = heads_q(h, i), heads_k(h, w)
            e2 = extra(h, i, w) if extra else None
            m = PE(lambda e: e.matmul(b.ap[:, 0:w], q, k, start=True, stop=e2 is None), ready, b.free)
            seen = mask_ready.get(i) if mask else None
            if e2:
                l2, r2, tok = e2
                m = PE(lambda e: e.matmul(b.ap[:, 0:w], l2, r2, start=False, stop=True), tok)
                extra_free(h, m)
            mk = mask(i, w) if mask else None
            if mk is not None:
                d = DVE(lambda e: e.tensor_tensor_reduce(pb.ap[:, 0:w], b.ap[:, 0:w], mk, -scale, 3e38, ALU.add, ALU.min, st.ap[:, 0:1]),
                        m, seen, pb.free, st.free)
            else:
                d = DVE(lambda e: e.tensor_scalar(pb.ap[:, 0:w], b.ap[:, 0:w], -scale, None, ALU.mult, ALU.min, accum_out=st.ap[:, 0:1]),
                        m, pb.free, st.free)
            b.free = [d]
            a = ACT(lambda e: e.activation(pb.ap[:, 0:w], pb.ap[:, 0:w], ACT_F.Exp, bias=st.ap[:, 0:1], scale=-1.0, accum_out=st.ap[:, 1:2]), d)
            prob[n] = a

        def divide(n):
            w = width(steps[n][1])
            pb, st = PB[n % len(PB)], stat[n % len(stat)]
            d = DVE(lambda e: e.reciprocal(st.ap[:, 2:3], st.ap[:, 1:2]), prob[n])
            g = DVE(lambda e: e.tensor_scalar(pb.ap[:, 0:w], pb.ap[:, 0:w], st.ap[:, 2:3], None, ALU.mult), d)
            st.free = [g]
            prob[n] = g

        def turn(n):
            h, i = steps[n]
            w = width(i)
            b, pb, pt = banks[(3, 4, 7)[n % 3]], PB[n % len(PB)], PT[h % 2]
            for j in range(0, w, P):
                m = PE(lambda e, j=j: e.transpose(b.ap[:, j:j + P], pb.ap[:, j:j + P], ident[:]), prob[n], b.free)
            pb.free = [m]
            dst = pt.ap[:, 0:w // P, i * P:(i + 1) * P]
            src = b.ap[:, 0:w].rearrange("p (j q) -> p j q", q=P)
            if n % 4:
                v = ACT(lambda e: e.activation(dst, src, ACT_F.Copy), m, pt.free)
            else:
                v = DVE(lambda e: e.tensor_copy(dst, src), m, pt.free)
            b.free = [v]
            if i == 0:
                pt.ready = []
            pt.ready.append(v)

        def values(h, j):
            b, pt = banks[5 + (h // 2) % 2], PT[h % 2]
            o = 64 * (h % 2)
            full = width(0) == S
            q0 = 0 if full else j * P
            v = heads_v(h, j)
            m = PE(lambda e: e.matmul(b.ap[o:o + 64, q0:S], v, pt.ap[:, j, q0:S], start=(j == 0), stop=(j == NT - 1)), pt.ready, b.free)
            pt.free = [m]
            if h % 2 and j == NT - 1:
                c = h // 2
                a = ACT(lambda e: e.activation(x.hi[:, c, :], b.ap[:], ACT_F.Copy), m, write_after)
                d = DVE(lambda e: e.tensor_tensor(x.lo[:, c, :], b.ap[:], x.hi[:, c, :].bitcast(F32), ALU.subtract), a)
                b.free = [d]
                x.ready[c] = [a, d]

        for n in range(len(steps) + LAG + 4):
            if LAG <= n < len(steps) + LAG:
                turn(n - LAG)
            if n < len(steps):
                if between:
                    between(n)
                scores(n)
            if 1 <= n < len(steps) + 1:
                divide(n - 1)
            for h, j in values_at.get(n, ()):
                values(h, j)

    extra_hook = [None]

    def extra_free(h, m):
        extra_hook[0](h, m)

    with ExitStack() as region:
        XT = sb("XT", [P, NT, D], F32, region)
        junk = sb("junk", [P, D], F32, region)
        R1, R2 = acc[0].ap[0:114, 0:P], acc[1].ap[0:96, 0:P]
        vec_loads = []
        s_g0 = sem("gain_in")
        s_x = [sem(f"x_in{i}") for i in range(NT)]
        xin = [SP.load(s_x[i], lambda e, i=i: e.dma_start(XT[:, i, :], t["x"][0, i * P:(i + 1) * P, :])) for i in range(NT)]
        for i in range(NT):
            a = ACT(lambda e: e.activation(junk[:], XT[:, i, :], ACT_F.Square, accum_out=rcol[:, i:i + 1]), xin[i], ACT.last())
        a = ACT(lambda e: e.activation(rcol[:, 0:NT], rcol[:, 0:NT], ACT_F.Sqrt, bias=eps[:, 0:1], scale=1.0 / D), d_const, a)
        root = DVE(lambda e: e.reciprocal(rcol[:, NT:2 * NT], rcol[:, 0:NT]), a)
        VEC = {}
        row = 0
        for names, src, n in (
            (("g_attn_a",), t["g_attn_a"][0], 8), (("g_kv",), t["g_kv"], 8), (("g_attn_b",), t["g_attn_b"][0], 8),
            (("g_mlp0", "g_mlp1"), t["g_mlp"], 8), (("g_final",), t["g_final"], 8),
            (("n1_0", "n1_1"), t["norm1_g_2"], 8), (("n2_0", "n2_1"), t["norm2_g_2"], 8),
            (("c",), t["c_2"][0], 8), (("b_in",), t["gmlp_b_in_2"][0, 0:3072], 24),
        ):
            for k, name in enumerate(names):
                VEC[name] = V1[:, row + k * n:row + (k + 1) * n]
            n *= len(names)
            flat_src = src.rearrange("(r k) -> r k", k=P) if len(names) == 1 else src.rearrange("l (r k) -> (l r) k", k=P)
            vec_loads.append((R1[row:row + n, :], flat_src))
            row += n
        for name, src in (("qg", t["attn_q_norm_g_2"]), ("kg", t["attn_k_norm_g_2"])):
            for half in range(2):
                vec_loads.append((R1[row:row + 1, 64 * half:64 * half + 64], src))
            VEC[name] = V1[:, row:row + 1]
            row += 1
        vec_loads.append((R2, t["ada_b_2"].rearrange("l (r k) -> (l r) k", k=P)))
        vec_loads.append((bf[:], t["b_f"].partition_broadcast(P)))
        g_in = SP.load(s_g0, lambda e: e.dma_start(*vec_loads[0]))
        load_next()
        load_next()
        for dst, src in vec_loads[1:]:
            vec_in = SP.load(s_vec, lambda e, dst=dst, src=src: e.dma_start(dst, src))
        const(head_mean[:], "head_mean")
        const(perm[0][:], "perm_half")
        const(perm[1][:], "perm_pair")
        c_ready = const(one_hot[:], "one_hot")
        split_next()
        for c in range(KC):
            b = gemm_bank()
            for i in range(NT):
                m = PE(lambda e, i=i, c=c, b=b: e.transpose(b.ap[:, i * P:(i + 1) * P], XT[:, i, c * P:(c + 1) * P], ident[:]), xin[i], i_in, b.free)
            if c % 2:
                v = DVE(lambda e, c=c, b=b: e.tensor_copy(HT[:, c, :], b.ap[:]), m)
            else:
                v = ACT(lambda e, c=c, b=b: e.activation(HT[:, c, :], b.ap[:], ACT_F.Copy), m)
            b.free = [v]
            h_ready[c] = [v]
            if c == 3:
                spread(root, rcol[:, NT:2 * NT])
        m = PE(lambda e: e.transpose(banks[4].ap[:, 0:KC], R1[0:KC, :], ident[0:KC, 0:KC]), g_in, i_in)
        g_set = DVE(lambda e: e.tensor_copy(V1[:, 0:KC], banks[4].ap[:, 0:KC]), m)
        banks[4].free = [g_set]
        normed(X, VEC["g_attn_a"], None, [g_set, h_ready])
        v1_ready = []

        def turn_vectors():
            b = banks[4]
            m = PE(lambda e: e.transpose(b.ap[:, 0:114], R1, ident[0:114, 0:114]), vec_in, g_in, b.free)
            d = DVE(lambda e: e.tensor_copy(V1[:, KC:114], b.ap[:, KC:114]), m)
            b.free = [d]
            v1_ready.append(d)
            b = banks[5]
            m = PE(lambda e: e.transpose(b.ap[:, 0:96], R2, ident[0:96, 0:96]), vec_in)
            d = DVE(lambda e: e.tensor_copy(V2[:], b.ap[:, 0:96]), m)
            b.free = [d]
            v2_ready.append(d)
            acc[0].free, acc[1].free = [v1_ready], [d]
            silu()
        defer(3, turn_vectors)
        def silu():
            a = ACT(lambda e: e.activation(cond[:, 0, :], VEC["c"], ACT_F.Exp, scale=-1.0), v1_ready)
            d = DVE(lambda e: e.tensor_scalar(cond[:, 0, :], cond[:, 0, :], 1.0, None, ALU.add), a)
            d = DVE(lambda e: e.reciprocal(cond[:, 1, :], cond[:, 0, :]), d)
            d = DVE(lambda e: e.tensor_tensor(cond[:, 2, :], cond[:, 1, :], VEC["c"], ALU.mult), d)
            cond_ready.append(d)

    s_rope = sem("rope_in")
    with ExitStack() as region:
        free = phase_end()
        Q = sb("QA", [P, KC, S], F32, region)
        K2 = [sb(f"KA{i}", [P, S], F32, region) for i in range(4)]
        V = sb("VA", [P, NT, 256], F32, region)
        PB = [Buf(sb(f"PA{i}", [P, S], F32, region), free) for i in range(5)]
        PT = [Buf(sb(f"PTA{i}", [P, NT, S], F32, region), free) for i in range(2)]
        QI = sb("QI", [P, 4, S], F32, region)
        KI = sb("KI", [P, S], F32, region)
        WI = sb("WI", [P, NT, 8], F32, region)
        SC = [Buf(sb(f"SC{i}", [P, S], F32, region), free) for i in range(3)]
        SC2 = Buf(sb("SCW", [P, S], F32, region), free)
        top = Buf(sb("top", [P, 8], F32, region), free)
        M = [sb(f"MA{i}", [P, (i + 1) * P], F32, region) for i in range(NT)]
        rope[0] = Buf(sb("rope_a", [P, 2, S], F32, region))
        rope[0].ready = [SP.load(s_rope, lambda e: e.dma_start(rope[0].ap[:], consts["rope_a"]))]
        i_ready, a_ready = [free], []
        qi_ready = [[] for _ in range(4)]
        DVE(lambda e: e.memset(M[0][:], 0.0), free)
        mask_ready[0] = [DVE(lambda e: e.memset(M[0][0:64, 64:128], -BIG), DVE.last())]

        def evac_qi(first):
            def evac(o, b, m):
                q, a = copy_out(b, m)
                c = first + o
                defer(1, lambda: rotate(q, a, 0, P, add_into(QI[:, c, :], qi_ready[c])))
            return evac
        DVE(lambda e: e.memset(top.ap[:], 0.0), free)
        gemm_fm("qi", X, 256, evac_qi(0), first=True)

        def evac_ki(o, b, m):
            q, a = copy_out(b, m, 72)
            bw = banks[6]

            def finish():
                for i in range(NT):
                    mt = PE(lambda e, i=i: e.transpose(bw.ap[:, 8 * i:8 * i + 8], q.ap[64:72, i * P:(i + 1) * P], ident[64:72, 64:72]), a, bw.free)
                w = DVE(lambda e: e.tensor_scalar(WI[:], bw.ap[:, 0:32].rearrange("p (i h) -> p i h", h=8),
                                                  8 ** -0.5 * 64 ** -0.5, None, ALU.mult), mt)
                bw.free = [w]
                i_ready.append(w)
                rotate(q, [a, mt], 0, 64, lambda x1, x2, rdy: ki_add(x1, x2, rdy))

            def ki_add(x1, x2, rdy):
                for half in range(2):
                    d = DVE(lambda e, half=half: e.tensor_tensor(KI[64 * half:64 * half + 64, :], x1.ap[0:64, :], x2.ap[0:64, :], ALU.add), rdy)
                i_ready.append(d)
                return d
            defer(1, finish)
        gemm_fm("ki", X, 72, evac_ki)
        gemm_fm("qj", X, 256, evac_qi(2))

        def evac_qa(o, b, m):
            q, a = copy_out(b, m)
            defer(1, lambda: rotate(q, a, 0, P, add_into(Q[:, o, :], a_ready, POOL)))
            select_some(6.2)

        def select():
            for i in range(1, NT):
                w = (i + 1) * P
                s = SC[i - 1]
                for h in range(8):
                    b = banks[5 + h % 3]
                    o = 64 * (h % 2)
                    m = PE(lambda e, h=h, o=o, i=i, w=w: e.matmul(b.ap[:, 0:w], QI[o:o + 64, h // 2, i * P:(i + 1) * P], KI[o:o + 64, 0:w],
                                                         start=True, stop=True), i_ready, qi_ready[h // 2], b.free)
                    q = scratch()
                    a = ACT(lambda e, q=q, w=w: e.activation(q.ap[:, 0:w], b.ap[:, 0:w], ACT_F.Relu), m, q.free)
                    b.free = [a]
                    if h == 0:
                        d = DVE(lambda e, q=q, i=i, h=h, w=w, s=s: e.tensor_scalar(s.ap[:, 0:w], q.ap[:, 0:w], WI[:, i, h:h + 1], None, ALU.mult), a, s.free)
                    else:
                        d = DVE(lambda e, q=q, i=i, h=h, w=w, s=s: e.scalar_tensor_tensor(
                            s.ap[:, 0:w], q.ap[:, 0:w], WI[:, i, h:h + 1], s.ap[:, 0:w], ALU.mult, ALU.add), a, d)
                    q.free = [d]
                    yield 0.25 + w / 1200
                d = DVE(lambda e, s=s, w=w: e.memset(s.ap[0:64, w - 64:w], SHUT), d)
                x1, x2 = s, SC2
                for _ in range(16):
                    d = DVE(lambda e, x1=x1, w=w: e.max(top.ap[:], x1.ap[:, 0:w]), d)
                    d = DVE(lambda e, x1=x1, x2=x2, w=w: e.match_replace(x2.ap[:, 0:w], top.ap[:], x1.ap[:, 0:w], USED), d)
                    x1, x2 = x2, x1
                    yield 0.26 + w / 426
                d = DVE(lambda e, i=i, w=w, x1=x1: e.tensor_scalar(M[i][:], x1.ap[:, 0:w], USED, -BIG, ALU.not_equal, ALU.mult), d, free)
                mask_ready[i] = [d]
                yield 0.3

        selecting = [None]

        def select_some(share=1e9, until=None):
            if selecting[0] is None:
                selecting[0] = select()
            while share > 0 and until not in mask_ready:
                cost = next(selecting[0], None)
                if cost is None:
                    return
                share -= cost
        gemm_fm("qa", X, 1024, evac_qa)

        def evac_ka(o, b, m):
            q, a = copy_out(b, m)
            defer(1, lambda: rotate(q, a, 0, P, add_twice([K2[2 * o], K2[2 * o + 1]], a_ready), DVE))
            select_some(4.4)
        gemm_fm("ka", X, 256, evac_ka)

        def evac_va(i, at, k, b, m):
            a = ACT(lambda e: e.activation(V[:, i, at:at + k], b.ap[:, 0:k], ACT_F.Copy), m, free)
            b.free = [a]
            a_ready.append(a)
            select_some(2.2)
        gemm_tm("va", X, 256, evac_va)
        tick(force=True)
        select_some(until=2)
        attention(
            lambda h, i: Q[64 * (h % 2):64 * (h % 2) + 64, h // 2, i * P:(i + 1) * P],
            lambda h, w: K2[h // 4][64 * (h % 2):64 * (h % 2) + 64, 0:w],
            lambda h, j: V[:, j, 64 * (h // 4):64 * (h // 4) + 64],
            lambda i, w: M[i][:, 0:w], lambda i: (i + 1) * P, None, a_ready, X, PB, PT,
            [(0, 0), (0, 1), (0, 2), (1, 0), (1, 1), (1, 2), (0, 3), (1, 3)] + [(h, i) for h in range(2, 16) for i in range(NT)],
            lambda n: select_some(2.1) if n < 6 else select_some())
        gemm_fm("oa", X, 1024, lambda o, b, m: add_to_h(o, b, m), first=True)
        tick(force=True)
        end_of_a = phase_end()

    mean_square()
    normed(X, VEC["g_mlp0"], None, [v1_ready, h_ready])
    mlp("m0")
    tick(force=True)

    with ExitStack() as region:
        mean_square()
        free = phase_end()
        Q = sb("QB", [P, KC, S], F32, region)
        K = sb("KB", [P, KC, S], F32, region)
        V = sb("VB", [P, NT, D], F32, region)
        PB = [Buf(sb(f"PBB{i}", [P, S], F32, region), free) for i in range(5)]
        PT = [Buf(sb(f"PTB{i}", [P, NT, S], F32, region), free) for i in range(2)]
        tsum = sb("tsum", [P, S], F32, region)
        LF = sb("LF", [P, 4, NT * 16], F32, region)
        CK = sb("CK", [P, S], F32, region)
        CQ = sb("CQ", [P, S], F32, region)
        MH = [Buf(sb(f"MH{i}", [P, S], F32, region), free) for i in range(2)]
        mask_ready.clear()
        s_tsum = sem("tsum_in")
        tri = sb("tri", [P, S], F32, region)
        SP.load(s_tsum, lambda e: e.dma_start(tri[:], consts["tri"]), end_of_a)
        tsum_in = SP.load(s_tsum, lambda e: e.dma_start(tsum[:], consts["tsum"]), end_of_a)
        normed(X, VEC["g_kv"], None, [v1_ready, h_ready])
        keep_rows()
        POOL(lambda e: e.memset(CK[:], 0.0), free, POOL.last())
        for o in (32, 96):
            POOL(lambda e: e.memset(CK[o:o + 16, :], 1.0), POOL.last())
        POOL(lambda e: e.memset(CQ[:], 0.0), POOL.last())
        for o in (0, 64):
            c_set = POOL(lambda e: e.memset(CQ[o:o + 16, :], 1.0), POOL.last())
        POOL.wait([c_set])
        f_ready, b_ready = [], [free]

        def evac_f(i, at, k, b, m):
            d = DVE(lambda e: e.tensor_tensor(LF[:, 0, 16 * i:16 * i + 16], b.ap[:, 0:16], bf[:], ALU.add), m, free)
            b.free = [d]
            f_ready.append(d)
        def keep(dst):
            def evac(o, b, m):
                a = ACT(lambda e: e.activation(dst[:, o, :], b.ap[:], ACT_F.Copy), m, free)
                b.free = [a]
                b_ready.append(a)
            return evac
        gemm_fm("kb", X, 1024, keep(K), first=True)
        gemm_tm("fb", X, 16, evac_f)
        d0 = DVE(lambda e: e.tensor_scalar(LF[:, 1, :], LF[:, 0, :], 0.0, None, ALU.min), f_ready)
        a = ACT(lambda e: e.activation(LF[:, 2, :], LF[:, 0, :], ACT_F.Abs), f_ready)
        a = ACT(lambda e: e.activation(LF[:, 3, :], LF[:, 2, :], ACT_F.Exp, scale=-1.0), a)
        d = DVE(lambda e: e.tensor_scalar(LF[:, 2, :], LF[:, 3, :], 1.0, None, ALU.add), a)
        a = ACT(lambda e: e.activation(LF[:, 3, :], LF[:, 2, :], ACT_F.Ln), d)
        d_lf = DVE(lambda e: e.tensor_tensor(LF[:, 0, :], LF[:, 1, :], LF[:, 3, :], ALU.subtract), a, d0)

        def running_sum():
            b = banks[6]
            for i in range(NT):
                m = PE(lambda e, i=i: e.matmul(b.ap[0:16, P * i:S], LF[:, 0, 16 * i:16 * i + 16], tsum[:, 0:S - P * i],
                                               start=(i == 0), stop=(i == NT - 1)), d_lf, tsum_in, b.free)
            for o in (32, 96):
                a = ACT(lambda e: e.activation(CQ[o:o + 16, :], b.ap[0:16, :], ACT_F.Copy, scale=8.0), m, c_set)
            for o in (0, 64):
                d = DVE(lambda e: e.tensor_scalar(CK[o:o + 16, :], b.ap[0:16, :], -8.0, None, ALU.mult), m, a)
            b.free = [d]
            b_ready.extend([a, d])
        defer(4, running_sum)


        def evac_vb(i, at, k, b, m):
            a = ACT(lambda e: e.activation(V[:, i, at:at + k], b.ap[:, 0:k], ACT_F.Copy), m, free)
            b.free = [a]
            b_ready.append(a)
        gemm_tm("vb", X, 1024, evac_vb)
        normed(X, VEC["g_attn_b"], None, [v1_ready, h_ready], rstd)
        gemm_fm("qb", X, 1024, keep(Q), first=True)
        tick(force=True)

        def decay(h, i, w):
            mh, o = MH[h % 2], 64 * (h % 2)
            if i == 0:
                g = POOL(lambda e: e.tensor_scalar(mh.ap[:], CK[:], one_hot[:, h:h + 1], None, ALU.mult), b_ready, mh.free, c_ready)
                mh.ready = [g]
                mh.free = []
            return CQ[o:o + 48, i * P:(i + 1) * P], mh.ap[o:o + 48, 0:w], mh.ready

        def used_decay(h, m):
            MH[h % 2].free = [m]
        extra_hook[0] = used_decay
        attention(
            lambda h, i: Q[64 * (h % 2):64 * (h % 2) + 64, h // 2, i * P:(i + 1) * P],
            lambda h, w: K[64 * (h % 2):64 * (h % 2) + 64, h // 2, 0:w],
            lambda h, j: V[:, j, 64 * h:64 * h + 64],
            lambda i, w: tri[:, 384 - i * P:384 - i * P + w], lambda i: (i + 1) * P, decay, [b_ready, tsum_in], X, PB, PT)
        gemm_fm("ob", X, 1024, lambda o, b, m: add_to_h(o, b, m), first=True)
        tick(force=True)

    gm_ready = []

    def mod_gains(layer):
        for k, norm in ((0, "n1"), (1, "n2")):
            sc = MOD[layer][:, 8 + 24 * k:16 + 24 * k]
            d = DVE(lambda e, sc=sc, k=k, norm=norm: e.scalar_tensor_tensor(GM[:, 2 * layer + k, :], sc, 1.0, VEC[f"{norm}_{layer}"], ALU.add, ALU.mult),
                    mod_ready[layer], v1_ready)
        if layer == 0:
            d = DVE(lambda e: e.tensor_tensor(FG[:], GM[:, 0, :], VEC["g_final"], ALU.mult), d, v1_ready)
        gm_ready.append(d)

    def mod(layer, k):
        return MOD[layer][:, 8 * k:8 * k + 8]

    mean_square()
    normed(X, VEC["g_mlp1"], None, [v1_ready, h_ready])
    mlp("m1", at_end=lambda: (mod_gains(0), mod_gains(1)))
    tick(force=True)
    m, b = PE.last(), banks[6]
    a = ACT(lambda e: e.activation(rcol[:, 0:NT], b.ap[:, 0:NT], ACT_F.Sqrt, bias=eps[:, 0:1]), m)
    d = DVE(lambda e: e.reciprocal(rcol[:, NT:2 * NT], rcol[:, 0:NT]), a)
    d2 = DVE(lambda e: e.tensor_tensor(r2[:, 0:NT], b.ap[:, NT:2 * NT], rcol[:, NT:2 * NT], ALU.mult), d)
    b.free = [d2]
    d2 = DVE(lambda e: e.tensor_tensor(r2[:, 0:NT], r2[:, 0:NT], rcol[:, NT:2 * NT], ALU.mult), d2)
    a = ACT(lambda e: e.activation(r2[:, 0:NT], r2[:, 0:NT], ACT_F.Sqrt, bias=eps[:, 0:1]), d2)
    d2 = DVE(lambda e: e.reciprocal(r2[:, NT:2 * NT], r2[:, 0:NT]), a)
    d2 = DVE(lambda e: e.tensor_tensor(r2[:, 0:NT], r2[:, NT:2 * NT], rcol[:, NT:2 * NT], ALU.mult), d2)
    spread(d2, r2[:, 0:NT])
    z_rows = to_rows(banks[5], d, rcol[:, NT:2 * NT])

    normed(X, FG, mod(0, 0), [gm_ready, h_ready])

    def turn_to_z(c):
        d = DVE(lambda e: e.scalar_tensor_tensor(HT[:, c, :], HT[:, c, :], VEC["g_final"][:, c:c + 1], banks[5].ap[:], ALU.mult, ALU.mult),
                z_rows, v1_ready, h_ready[c])
        h_ready[c] = [d]
        banks[5].free = [d]
    for c in range(KC):
        defer(3 + c, lambda c=c: turn_to_z(c))
    with ExitStack() as region:
        free = phase_end()
        rope[0] = Buf(sb("rope_b", [P, 2, S], F32, region))
        rope[0].ready = [SP.load(s_rope, lambda e: e.dma_start(rope[0].ap[:], consts["rope_b"]), free)]
        Q = sb("QC", [P, KC, S], F32, region)
        K2 = [sb(f"KC{i}", [P, S], F32, region) for i in range(4)]
        V = sb("VC", [P, NT, 256], F32, region)
        PB = [Buf(sb(f"PC{i}", [P, S], F32, region), free) for i in range(5)]
        PT = [Buf(sb(f"PTC{i}", [P, NT, S], F32, region), free) for i in range(2)]
        a_ready = [free]

        def head_norm(gain, done):
            def evac(o, b, m):
                q, a = copy_out(b, m)

                def norm():
                    r = scratch()
                    s = ACT(lambda e: e.activation(r.ap[:], q.ap[:], ACT_F.Square), a, r.free)
                    bm = banks[6]
                    mm = PE(lambda e: e.matmul(bm.ap[:], head_mean[:], r.ap[:], start=True, stop=True), s, bm.free)
                    s = ACT(lambda e: e.activation(r.ap[:], bm.ap[:], ACT_F.Sqrt, bias=eps[:, 0:1]), mm)
                    bm.free = [s]
                    d = DVE(lambda e: e.reciprocal(r.ap[:], r.ap[:]), s)
                    d = DVE(lambda e: e.scalar_tensor_tensor(q.ap[:], q.ap[:], gain, r.ap[:], ALU.mult, ALU.mult), d)
                    r.free = [d]
                    defer(2, lambda: rotate(q, d, 1, P, done(o)))
                defer(1, norm)
            return evac
        gemm_fm("kc", X, 256, head_norm(VEC["kg"], lambda o: add_twice([K2[2 * o], K2[2 * o + 1]], a_ready)), first=True)

        def evac_vc(i, at, k, b, m):
            a = ACT(lambda e: e.activation(V[:, i, at:at + k], b.ap[:, 0:k], ACT_F.Copy), m, free)
            b.free = [a]
            a_ready.append(a)
        gemm_fm("qc", X, 1024, head_norm(VEC["qg"], lambda o: add_into(Q[:, o, :], a_ready)))
        gemm_tm("vc", X, 256, evac_vc)
        tick(force=True)
        attention(
            lambda h, i: Q[64 * (h % 2):64 * (h % 2) + 64, h // 2, i * P:(i + 1) * P],
            lambda h, w: K2[h // 4][64 * (h % 2):64 * (h % 2) + 64, 0:w],
            lambda h, j: V[:, j, 64 * (h // 4):64 * (h // 4) + 64],
            None, lambda i: S, None, a_ready, X, PB, PT)
        gemm_fm("oc", X, 1024, lambda o, b, m: add_to_h(o, b, m, mod(0, 2)), first=True)
        tick(force=True)
    mean_square()
    normed(X, GM[:, 1, :], mod(0, 3), [gm_ready, h_ready])
    mlp("m2", mod(0, 5))
    tick(force=True)
    mean_square()
    normed(X, GM[:, 2, :], mod(1, 0), [gm_ready, h_ready])
    with ExitStack() as region:
        free = phase_end()
        VT = sb("VT", [P, NT, 3072], F32, region)
        wsT = sb("wsT", [P, 16, P], F32, region)
        sums = acc[0].ap[0:16, :]
        LNV = sb("LNV", [P, 48], F32, region)
        s_g, s_l = sem("gmlp_in"), sem("ln_in")
        with ExitStack() as sub:
            row_a = Buf(sb("row_a", [P, 3072], F32, sub))
            s_a = sem("row_a_in")
            row_a.ready = [SP.load(s_a, lambda e: e.dma_start(row_a.ap[:], t["gmlp_b_in_2"][0, 3072:6144].partition_broadcast(P)), free)]
            bs_in = SP.load(s_g, lambda e: e.dma_start(sums[:, P:2 * P], t["gmlp_b_s_2"][0]), free)
            s_w = [sem(f"ws_in{i}") for i in range(2)]
            turned = []

            def turn_ws(k):
                w = tmp[k % 2]
                ld = SP.load(s_w[k % 2], lambda e: e.dma_start(
                    w.ap[:].rearrange("p (g q) -> p g q", q=P),
                    t["gmlp_w_s_2"][0, 4 * k:4 * k + 4].rearrange("g p q -> p g q")), w.free)

                def turn_now():
                    b = banks[4 + k % 2]
                    for g in range(4):
                        m = PE(lambda e: e.transpose(b.ap[:, g * P:(g + 1) * P], w.ap[:, g * P:(g + 1) * P], ident[:]), ld, b.free)
                    w.free = [m]
                    d = DVE(lambda e: e.tensor_copy(wsT[:, 4 * k:4 * k + 4, :].rearrange("p g q -> p (g q)"), b.ap[:]), m, free)
                    b.free = [d]
                    turned.append(d)
                defer(6, turn_now)
            for k in range(4):
                defer(4 + 8 * k, lambda k=k: turn_ws(k))

            def load_ln():
                w = tmp[2]
                for k, src in enumerate((t["gmlp_ln_g_2"][0], t["gmlp_ln_b_2"][0])):
                    ld = SP.load(s_l, lambda e: e.dma_start(w.ap[24 * k:24 * k + 24, 0:P], src.rearrange("(r k) -> r k", k=P)), w.free)

                def turn_ln():
                    b = banks[4]
                    m = PE(lambda e: e.transpose(b.ap[:, 0:48], w.ap[0:48, 0:P], ident[0:48, 0:48]), ld, b.free)
                    w.free = [m]
                    d = DVE(lambda e: e.tensor_copy(LNV[:], b.ap[:, 0:48]), m, free)
                    b.free = [d]
                    turned.append(d)
                defer(6, turn_ln)
            defer(38, load_ln)

            def sum_rows():
                b, w = banks[5], tmp[3]
                for g in range(16):
                    m = PE(lambda e, g=g: e.matmul(b.ap[:, g:g + 1], wsT[:, g, :], ones[:, 0:1], start=True, stop=True), turned, b.free)
                d = DVE(lambda e: e.tensor_copy(w.ap[:, 0:16], b.ap[:, 0:16]), m, w.free)
                m = PE(lambda e: e.transpose(b.ap[0:16, 0:P], w.ap[:, 0:16], ident[:]), d)
                w.free = [m]
                d = DVE(lambda e: e.tensor_copy(sums[:, 0:P], b.ap[0:16, 0:P]), m, free)
                b.free = [d]
                turned.append(d)
            defer(46, sum_rows)
            v_ready = [[] for _ in range(NT)]

            def evac_gv(i, at, k, b, m):
                d = DVE(lambda e: e.tensor_tensor(VT[:, i, at:at + k], b.ap[:, 0:k], row_a.ap[:, at:at + k], ALU.add), m, row_a.ready)
                b.free = [d]
                a = ACT(lambda e: e.activation(VT[:, i, at:at + k], VT[:, i, at:at + k], ACT_F.Gelu), d)
                v_ready[i].append(a)
                if at % 512:
                    s = DVE(lambda e, f=at // 512: e.bn_stats(bst[:, i, f, :], VT[:, i, 512 * f:512 * f + 512]), v_ready[i])
                    v_ready[i] = [s]
            gemm_tm("gv", X, 3072, evac_gv)
            for i in range(NT):
                d = DVE(lambda e, i=i: e.bn_aggr(mv[:, i, :], bst[:, i, :, :]), v_ready[i])
            a = ACT(lambda e: e.activation(rsv[:], mv[:, :, 1], ACT_F.Sqrt, bias=eps[:, 0:1]), d)
            d = DVE(lambda e: e.reciprocal(rsv[:], rsv[:]), a)
            d = DVE(lambda e: e.scalar_tensor_tensor(nmr[:], mv[:, :, 0], -1.0, rsv[:], ALU.mult, ALU.mult), d)
            vn = []
            for f in range(6):
                for i in range(NT):
                    z = VT[:, i, 512 * f:512 * f + 512]
                    if i == 3:
                        vn.append(ACT(lambda e: e.activation(z, z, ACT_F.Identity, bias=nmr[:, i:i + 1], scale=rsv[:, i:i + 1]), d))
                    else:
                        vn.append(DVE(lambda e: e.tensor_scalar(z, z, rsv[:, i:i + 1], nmr[:, i:i + 1], ALU.mult, ALU.add), d))
        free = phase_end()
        Y = Split(sb("Yhi", [P, KC, S], F32R, region), sb("Ylo", [P, KC, S], F32R, region), free)

        def mix(j, q, a, write_after):
            b, b2, r, side = banks[4 + j % 2], banks[6 + j % 2], scratch(), scratch()
            parts = [(0, P, (P * j) // 192)] if (P * j) // 192 == (P * j + P - 1) // 192 else [
                (0, 64, (P * j) // 192), (64, 64, (P * j + 64) // 192)]
            for o, rows, g in parts:
                for i in range(NT):
                    m = PE(lambda e: e.matmul(
                        b.ap[o:o + rows, i * P:(i + 1) * P], VT[:, i, P * j + o:P * j + o + rows], wsT[:, g, :],
                        start=True, stop=True), b.free, vn[NT * (j // 4):NT * (j // 4) + NT], turned)
                m2 = PE(lambda e: e.matmul(b2.ap[o:o + rows, 0:2 * P], ident[0:16, g:g + 1].to_broadcast([16, rows]), sums,
                                           start=True, stop=True), b2.free, bs_in)
            d = DVE(lambda e: e.tensor_copy(side.ap[:, 0:P], b2.ap[:, P:2 * P]), m2, side.free)
            d = DVE(lambda e: e.scalar_tensor_tensor(side.ap[:, 0:P], b2.ap[:, 0:P], LNV[:, 24 + j:25 + j], side.ap[:, 0:P], ALU.mult, ALU.add), d)
            b2.free = [d]
            d = DVE(lambda e: e.scalar_tensor_tensor(
                r.ap[:].rearrange("p (i q) -> p i q", q=P), b.ap[:].rearrange("p (i q) -> p i q", q=P), LNV[:, j:j + 1],
                side.ap[:, 0:P].unsqueeze(1).to_broadcast([P, NT, P]), ALU.mult, ALU.add), m, m2, d, r.free)
            side.free = [d]
            b.free = [d]
            d = DVE(lambda e: e.tensor_tensor(q.ap[:], r.ap[:], q.ap[:], ALU.mult), d, a)
            r.free = [d]
            c = j % 8
            a2 = ACT(lambda e: e.activation(Y.hi[:, c, :], q.ap[:], ACT_F.Copy), d, write_after)
            d = DVE(lambda e: e.tensor_tensor(Y.lo[:, c, :], q.ap[:], Y.hi[:, c, :].bitcast(F32), ALU.subtract), a2)
            q.free = [d]
            Y.ready[c] = [a2, d]
        for g in range(3):
            write_after = list(Y.free)

            def evac_gu(o, b, m, g=g, write_after=write_after):
                q = hold()
                j = 8 * g + o
                a = ACT(lambda e: e.activation(q.ap[:], b.ap[:], ACT_F.Gelu, bias=VEC["b_in"][:, j:j + 1]), m, q.free)
                b.free = [a]
                defer(2, lambda: mix(j, q, a, write_after))
            gemm_fm("gu", X, 1024, evac_gu)
            tick(force=True)
            gemm_fm("go", Y, 1024, lambda o, b, m: add_to_h(o, b, m, mod(1, 2), last=(g == 2)), first=True)
            tick(force=True)
    mean_square()
    normed(X, GM[:, 3, :], mod(1, 3), [gm_ready, h_ready])
    mlp("m3", mod(1, 5))
    tick(force=True)

    s_out = sem("out_done")
    with ExitStack() as region:
        free = phase_end()
        O = sb("O", [P, NT, D], F32, region)
        for i in range(NT):
            vs = []
            for half in range(2):
                b = gemm_bank()
                for c in range(4):
                    cc = 4 * half + c
                    m = PE(lambda e, c=c, cc=cc, i=i, b=b: e.transpose(b.ap[:, c * P:(c + 1) * P], HT[:, cc, i * P:(i + 1) * P], ident[:]), h_ready[cc], b.free)
                dst = O[:, i, 512 * half:512 * half + 512]
                if half:
                    v = DVE(lambda e, dst=dst, b=b: e.tensor_copy(dst, b.ap[:]), m, free)
                else:
                    v = ACT(lambda e, dst=dst, b=b: e.activation(dst, b.ap[:], ACT_F.Copy), m, free)
                b.free = [v]
                vs.append(v)
            o_done = SP.load(s_out, lambda e, i=i: e.dma_start(out[0, i * P:(i + 1) * P, :], O[:, i, :]), vs)
    SP.wait([o_done])


def shape_constants():
    f = np.float32
    i = np.arange(P)
    inv = (1.0 / (f(10000.0) ** (np.arange(0, 64, 2, dtype=f) / f(64)))).astype(f)
    ang = np.arange(S, dtype=f)[:, None] * inv[None, :]
    c, s = np.cos(ang).T.astype(f), np.sin(ang).T.astype(f)
    rope_a = np.stack([np.tile(c, (4, 1)), np.concatenate([-s, s, -s, s])], 1)
    perm_half = np.zeros((P, P), f)
    perm_half[i, i ^ 32] = 1
    perm_pair = np.zeros((P, P), f)
    perm_pair[i, i ^ 1] = 1
    tok = np.arange(S)
    row = (tok // 64 - (S // 64) // 2).astype(f)
    col = (tok % 64 - 32).astype(f)
    freq = (f(10000.0) ** (-np.arange(16, dtype=f) / f(16))).astype(f)
    ang = np.concatenate([row[:, None] * freq, col[:, None] * freq], -1)
    c, s = np.cos(ang).T.astype(f), np.sin(ang).T.astype(f)
    sign = np.where(i % 2, 1.0, -1.0).astype(f)[:, None]
    rope_b = np.stack([c[(i % 64) // 2], sign * s[(i % 64) // 2]], 1)
    tri = np.zeros((P, S), f)
    tri[:, 384:] = np.where(i[None, :] > i[:, None], -BIG, 0.0)
    tsum = np.ones((P, S), f)
    tsum[:, 0:P] = i[:, None] <= i[None, :]
    one_hot = np.tile(np.eye(32, 16, dtype=f), (4, 1))
    return {
        "ident": np.eye(P, dtype=f), "head_mean": np.kron(np.eye(2), np.full((64, 64), 1 / 64)).astype(f),
        "perm_half": perm_half, "perm_pair": perm_pair, "one_hot": one_hot,
        "rope_a": rope_a.astype(f), "rope_b": rope_b.astype(f), "tri": tri, "tsum": tsum,
    }


def kernel(**inputs):
    import numpy as _np
    import concourse.bacc as _bacc
    from concourse import mybir as _mybir
    from concourse.bass_utils import run_bass_kernel_spmd as _run

    nc = _bacc.Bacc("TRN2", target_bir_lowering=False, num_devices=1)
    arrays, t, consts = {}, {}, {}
    for name in inputs:
        a = _np.ascontiguousarray(inputs[name])
        arrays[f"in_{name}"] = a
        t[name] = nc.dram_tensor(f"in_{name}", a.shape, _mybir.dt.from_np(a.dtype), kind="ExternalInput").ap()
    for name, a in shape_constants().items():
        a = _np.ascontiguousarray(a)
        arrays[f"const_{name}"] = a
        consts[name] = nc.dram_tensor(f"const_{name}", a.shape, _mybir.dt.from_np(a.dtype), kind="ExternalInput").ap()
    out = nc.dram_tensor("out_0", (1, S, D), F32, kind="ExternalOutput").ap()
    program(nc, t, consts, out)
    r = _run(nc, [arrays], core_ids=[0])
    return r.results[0]["out_0"]
```
